# Optimizing a Trainium2 kernel written in Bass

```python
import math
import jax, jax.numpy as jnp
from jax import lax
import numpy as np

D_MODEL = 1024
BATCH = 1
SEQ = 256
DEPTH = 2

MOBA_HEADS = 8
MOBA_HEAD_DIM = 64
MOBA_WIDTH = MOBA_HEADS * MOBA_HEAD_DIM
MOBA_BLOCK = 256
MOBA_TOPK = 3
ROPE_THETA = 10000.0
RET_HEADS = 4
RET_QK_DIM = 128
RET_V_DIM = 256
RET_QK_WIDTH = RET_HEADS * RET_QK_DIM
RET_V_WIDTH = RET_HEADS * RET_V_DIM
RET_CHUNK = 256
PEER_N_KEYS = 128
PEER_N_EXPERTS = PEER_N_KEYS * PEER_N_KEYS
PEER_HEADS = 8
PEER_KEY_DIM = 256
PEER_TOPK = 16
PEER_TOKEN_CHUNK = 128
DN_ALPHA = (2.0 * DEPTH) ** 0.25
DN_BETA = (8.0 * DEPTH) ** -0.25
LN_EPS = 1e-5
NEG = -1e30

IN_SIZES = (MOBA_WIDTH, MOBA_WIDTH, MOBA_WIDTH, RET_QK_WIDTH, RET_QK_WIDTH, RET_V_WIDTH, RET_V_WIDTH, D_MODEL, D_MODEL)
IN_WIDTH = sum(IN_SIZES)
SPLIT_POINTS = tuple(int(v) for v in np.cumsum(IN_SIZES)[:-1])

kernel_name = 'hybrid_moba_retnet_peer_deepnorm'

def layer_norm(x, g, b):
    xf = x.astype(jnp.float32)
    mu = xf.mean(-1, keepdims=True)
    var = jnp.square(xf - mu).mean(-1, keepdims=True)
    return ((xf - mu) * lax.rsqrt(var + LN_EPS) * g.astype(jnp.float32) + b.astype(jnp.float32)).astype(x.dtype)

def group_norm(y):
    yf = y.astype(jnp.float32)
    mu = yf.mean(-1, keepdims=True)
    var = jnp.square(yf - mu).mean(-1, keepdims=True)
    return ((yf - mu) * lax.rsqrt(var + LN_EPS)).astype(y.dtype)

def rope_half(x, pos):
    d = x.shape[-1]
    inv = ROPE_THETA ** (-jnp.arange(0, d, 2, dtype=jnp.float32) / d)
    ang = pos[:, None] * inv[None, :]
    cos, sin = jnp.cos(ang), jnp.sin(ang)
    x1, x2 = x[..., : d // 2], x[..., d // 2:]
    return jnp.concatenate([x1 * cos - x2 * sin, x2 * cos + x1 * sin], axis=-1).astype(x.dtype)

def rotate_retnet(x, pos):
    d = x.shape[-1]
    inv = 1.0 / (ROPE_THETA ** jnp.linspace(0.0, 1.0, d // 2, dtype=jnp.float32))
    ang = pos[:, None] * inv[None, :]
    cos, sin = jnp.cos(ang), jnp.sin(ang)
    x1, x2 = x[..., 0::2], x[..., 1::2]
    return jnp.stack([x1 * cos - x2 * sin, x2 * cos + x1 * sin], axis=-1).reshape(x.shape).astype(x.dtype)

def moba_attention(q, k, v):
    B, H, S, d = q.shape
    nb = S // MOBA_BLOCK
    scale = d ** -0.5
    kb = k.reshape(B, H, nb, MOBA_BLOCK, d)
    vb = v.reshape(B, H, nb, MOBA_BLOCK, d)
    qb = jnp.moveaxis(q.reshape(B, H, nb, MOBA_BLOCK, d), 2, 0)
    k_mean = kb.astype(jnp.float32).mean(axis=3)
    n_sel = min(MOBA_TOPK, nb)
    causal = jnp.tril(jnp.ones((MOBA_BLOCK, MOBA_BLOCK), dtype=bool))
    b_ix = jnp.arange(B)[:, None, None, None]
    h_ix = jnp.arange(H)[None, :, None, None]
    blk_ids = jnp.arange(nb)
    slot_ids = jnp.arange(n_sel)

    def one_block(args):
        i, q_i = args
        gate = jnp.einsum('bhld,bhnd->bhln', q_i.astype(jnp.float32), k_mean)
        gate = jnp.where(blk_ids < i, gate, NEG)
        _, top_idx = lax.top_k(gate, n_sel)
        valid = slot_ids < i
        k_sel = kb[b_ix, h_ix, top_idx]
        v_sel = vb[b_ix, h_ix, top_idx]
        s_sel = jnp.einsum('bhld,bhlrkd->bhlrk', q_i, k_sel).astype(jnp.float32) * scale
        s_sel = jnp.where(valid[:, None], s_sel, NEG).reshape(B, H, MOBA_BLOCK, n_sel * MOBA_BLOCK)
        k_own = lax.dynamic_index_in_dim(kb, i, axis=2, keepdims=False)
        v_own = lax.dynamic_index_in_dim(vb, i, axis=2, keepdims=False)
        s_own = jnp.einsum('bhld,bhkd->bhlk', q_i, k_own).astype(jnp.float32) * scale
        s_own = jnp.where(causal, s_own, NEG)
        p = jax.nn.softmax(jnp.concatenate([s_sel, s_own], axis=-1), axis=-1).astype(v.dtype)
        p_sel = p[..., : n_sel * MOBA_BLOCK].reshape(B, H, MOBA_BLOCK, n_sel, MOBA_BLOCK)
        p_own = p[..., n_sel * MOBA_BLOCK:]
        return (jnp.einsum('bhlrk,bhlrkd->bhld', p_sel, v_sel)
                + jnp.einsum('bhlk,bhkd->bhld', p_own, v_own))

    out = lax.map(one_block, (blk_ids, qb))
    return jnp.moveaxis(out, 0, 2).reshape(B, H, S, d)

def retention(q, k, v):
    B, H, S, dk = q.shape
    dv = v.shape[-1]
    C = RET_CHUNK
    nc = S // C
    log_g = jnp.log(1.0 - 2.0 ** (-5.0 - jnp.arange(H, dtype=jnp.float32)))
    k = k * (dk ** -0.5)
    qc = q.reshape(B, H, nc, C, dk)
    kc = k.reshape(B, H, nc, C, dk)
    vc = v.reshape(B, H, nc, C, dv)
    pos = jnp.arange(C, dtype=jnp.float32)
    diff = pos[:, None] - pos[None, :]
    decay = jnp.where(diff >= 0, jnp.exp(log_g[:, None, None] * jnp.maximum(diff, 0.0)), 0.0)
    scores = jnp.einsum('bhncd,bhnmd->bhncm', qc, kc) * decay[None, :, None]
    y_inner = jnp.einsum('bhncm,bhnme->bhnce', scores, vc)
    k_decay = jnp.exp(log_g[:, None] * (C - 1.0 - pos))
    q_decay = jnp.exp(log_g[:, None] * (pos + 1.0))
    chunk_decay = jnp.exp(log_g * C)
    kv = jnp.einsum('bhncd,bhnce->nbhde', kc * k_decay[None, :, None, :, None], vc)

    def step(state, kv_n):
        return state * chunk_decay[None, :, None, None] + kv_n, state

    _, prev = lax.scan(step, jnp.zeros((B, H, dk, dv), kv.dtype), kv)
    y_cross = jnp.einsum('bhncd,nbhde->bhnce', qc, prev) * q_decay[None, :, None, :, None]
    return (y_inner + y_cross).reshape(B, H, S, dv)

def token_mixer(x, w_in, w_moba_out, w_ret_out, w_out):
    B, S, _ = x.shape
    pad = (-S) % MOBA_BLOCK
    Sp = S + pad
    proj = jnp.einsum('bsd,de->bse', x, w_in)
    q_a, k_a, v_a, q_r, k_r, v_r, g_r, gate_a, gate_r = jnp.split(proj, SPLIT_POINTS, axis=-1)

    def to_heads(t, n_heads):
        t = jnp.pad(t, ((0, 0), (0, pad), (0, 0)))
        return t.reshape(B, Sp, n_heads, -1).transpose(0, 2, 1, 3)

    pos = jnp.arange(Sp, dtype=jnp.float32)
    qa = rope_half(to_heads(q_a, MOBA_HEADS), pos)
    ka = rope_half(to_heads(k_a, MOBA_HEADS), pos)
    va = to_heads(v_a, MOBA_HEADS)
    y_a = moba_attention(qa, ka, va)[:, :, :S]
    y_a = y_a.transpose(0, 2, 1, 3).reshape(B, S, MOBA_WIDTH)

    qr = rotate_retnet(to_heads(q_r, RET_HEADS), pos)
    kr = rotate_retnet(to_heads(k_r, RET_HEADS), pos)
    vr = to_heads(v_r, RET_HEADS)
    y_r = group_norm(retention(qr, kr, vr)[:, :, :S])
    y_r = y_r.transpose(0, 2, 1, 3).reshape(B, S, RET_V_WIDTH)
    y_r = jax.nn.silu(g_r) * y_r

    branch_a = jnp.einsum('bse,ed->bsd', y_a, w_moba_out)
    branch_r = jnp.einsum('bse,ed->bsd', y_r, w_ret_out)
    merged = jax.nn.sigmoid(gate_a) * branch_a + jax.nn.sigmoid(gate_r) * branch_r
    return jnp.einsum('bsd,de->bse', merged, w_out)

def peer_ffn(x, w_query, sub_keys, expert_u, expert_v):
    B, S, D = x.shape
    L = PEER_TOKEN_CHUNK
    xt = x.reshape((B * S) // L, L, D)

    def one_chunk(xc):
        q = jnp.einsum('ld,de->le', xc, w_query).reshape(L, PEER_HEADS, 2, PEER_KEY_DIM // 2)
        s = jnp.einsum('lhpd,pkd->lhpk', q, sub_keys).astype(jnp.float32)
        s_top, i_top = lax.top_k(s, PEER_TOPK)
        cand_s = (s_top[:, :, 0, :, None] + s_top[:, :, 1, None, :]).reshape(L, PEER_HEADS, PEER_TOPK * PEER_TOPK)
        cand_i = (i_top[:, :, 0, :, None] * PEER_N_KEYS + i_top[:, :, 1, None, :]).reshape(L, PEER_HEADS, PEER_TOPK * PEER_TOPK)
        fin_s, fin_pos = lax.top_k(cand_s, PEER_TOPK)
        fin_i = jnp.take_along_axis(cand_i, fin_pos, axis=-1)
        g = jax.nn.softmax(fin_s, axis=-1).astype(xc.dtype)
        u = expert_u[fin_i]
        h = jax.nn.gelu(jnp.einsum('ld,lhkd->lhk', xc, u))
        v = expert_v[fin_i]
        return jnp.einsum('lhk,lhkd->ld', g * h, v)

    return lax.map(one_chunk, xt).reshape(B, S, D)

def setup_inputs(seed: int = 0) -> dict:
    key = jax.random.key(seed)
    ks = jax.random.split(key, 14)
    f32 = jnp.float32
    offsets = np.concatenate([[0], np.cumsum(IN_SIZES)])
    col_scale = np.ones((IN_WIDTH,), np.float32)
    col_scale[offsets[2]:offsets[3]] = DN_BETA
    col_scale[offsets[5]:offsets[6]] = DN_BETA
    x = jax.random.normal(ks[0], (BATCH, SEQ, D_MODEL), f32)
    w_in = jax.random.normal(ks[1], (DEPTH, D_MODEL, IN_WIDTH), f32) * (D_MODEL ** -0.5) * jnp.asarray(col_scale)
    w_moba_out = jax.random.normal(ks[2], (DEPTH, MOBA_WIDTH, D_MODEL), f32) * (MOBA_WIDTH ** -0.5) * DN_BETA
    w_ret_out = jax.random.normal(ks[3], (DEPTH, RET_V_WIDTH, D_MODEL), f32) * (RET_V_WIDTH ** -0.5) * DN_BETA
    w_out = jax.random.normal(ks[4], (DEPTH, D_MODEL, D_MODEL), f32) * (D_MODEL ** -0.5) * DN_BETA
    ln1_g = 1.0 + 0.02 * jax.random.normal(ks[5], (DEPTH, D_MODEL), f32)
    ln1_b = 0.02 * jax.random.normal(ks[6], (DEPTH, D_MODEL), f32)
    peer_w_query = jax.random.normal(ks[7], (DEPTH, D_MODEL, PEER_HEADS * PEER_KEY_DIM), f32) * (D_MODEL ** -0.5)
    peer_sub_keys = jax.random.normal(ks[8], (DEPTH, 2, PEER_N_KEYS, PEER_KEY_DIM // 2), f32) * ((PEER_KEY_DIM // 2) ** -0.5)
    peer_u = jax.random.normal(ks[9], (DEPTH, PEER_N_EXPERTS, D_MODEL), f32) * (D_MODEL ** -0.5)
    peer_v = jax.random.normal(ks[10], (DEPTH, PEER_N_EXPERTS, D_MODEL), f32) * DN_BETA
    ln2_g = 1.0 + 0.02 * jax.random.normal(ks[11], (DEPTH, D_MODEL), f32)
    ln2_b = 0.02 * jax.random.normal(ks[12], (DEPTH, D_MODEL), f32)
    return {'x': x, 'w_in': w_in, 'w_moba_out': w_moba_out, 'w_ret_out': w_ret_out, 'w_out': w_out,
            'ln1_g': ln1_g, 'ln1_b': ln1_b, 'peer_w_query': peer_w_query, 'peer_sub_keys': peer_sub_keys,
            'peer_u': peer_u, 'peer_v': peer_v, 'ln2_g': ln2_g, 'ln2_b': ln2_b}

def reference(x, w_in, w_moba_out, w_ret_out, w_out, ln1_g, ln1_b, peer_w_query, peer_sub_keys,
              peer_u, peer_v, ln2_g, ln2_b):
    for l in range(DEPTH):
        mix = token_mixer(x, w_in[l], w_moba_out[l], w_ret_out[l], w_out[l])
        x = layer_norm(DN_ALPHA * x + mix, ln1_g[l], ln1_b[l])
        ffn = peer_ffn(x, peer_w_query[l], peer_sub_keys[l], peer_u[l], peer_v[l])
        x = layer_norm(DN_ALPHA * x + ffn, ln2_g[l], ln2_b[l])
    return x


_drawn_inputs = setup_inputs


def setup_inputs(seed=0):
    import zlib

    import numpy as np

    out = dict(_drawn_inputs(seed))
    spreads = {}
    factors = {}
    for name, (base, spread) in spreads.items():
        noise = np.random.default_rng([zlib.crc32(name.encode()), seed]).standard_normal(out[name].shape)
        drawn = base * np.exp(spread * noise) if base else spread * noise
        out[name] = __import__('jax').numpy.asarray(drawn.astype(out[name].dtype))
    for name, factor in factors.items():
        out[name] = (out[name] * factor).astype(out[name].dtype)
    return out
```

```python
from contextlib import ExitStack

import concourse.bass as bass
from concourse import mybir

F32 = mybir.dt.float32
I32 = mybir.dt.int32
U32 = mybir.dt.uint32
ALU = mybir.AluOpType
ACT = mybir.ActivationFunctionType
AX_X = mybir.AxisListType.X

P = 128
D = 1024
KD = D // P
SEQ = 256
NT = SEQ // P
DEPTH = 2
IN_WIDTH = 6656
BLK = 512
MH, MD = 8, 64
RH, RK, RV = 4, 128, 256
PH, PK, NKEY, NSEL = 8, 128, 128, 16
NEXP = NKEY * NKEY
ALPHA = (2.0 * DEPTH) ** 0.25
EPS = 1e-5
SCALE = MD ** -0.5
GELU_C = 0.7978845608028654
GELU_A = 0.044715
LOWEST = -3.0e38
HEADS = NT * PH

UNITS = ([("in", n) for n in range(IN_WIDTH // BLK)]
         + [("moba", 0), ("ret", 0), ("moba", 1), ("ret", 1), ("out", 0), ("out", 1), ("keys", 0)]
         + [("query", n) for n in range(4)])
W_RING = 3
UNIT = KD * BLK
assert len(UNITS) % W_RING == 0
U_RING = 8
DIAGS = 4
QUERY_STEPS = ([(hp, (0,)) for hp in range(4)] + [(hp, (1,)) for hp in range(4)]
               + [(hp, (0, 1)) for hp in range(4, 2 * PH)])
FIRST_EXP = 9
IDX_BUFS = 3
assert (HEADS - 1) % IDX_BUFS == 0

D_FILLS = ([(b, t) for b in ("q_a", "k_a", "q_r") for t in range(NT)]
           + [("s0", g) for g in range(2)] + [("s1", g) for g in range(4)]
           + [("k_r", t) for t in range(NT)]
           + [("sc0", g) for g in range(2)] + [("sc1", g) for g in range(2)]
           + [(b, t) for b in ("g_r0", "g_r1") for t in range(NT)]
           + [("ya", t) for t in range(NT)]
           + [("yr", t, g) for t in range(NT) for g in range(2)]
           + [("br", hf, w, g) for hf in range(2) for w in range(2) for g in range(2)]
           + [("mix", hf, t) for t in range(NT) for hf in range(2)])
A_FILLS = ([("xT", t, g) for t in range(NT) for g in range(2)]
           + [("v_a", t) for t in range(NT)]
           + [(b, t) for b in ("qaT", "kaT") for t in range(NT)]
           + [(b, t) for b in ("v_r0", "v_r1") for t in range(NT)]
           + [(b, t) for b in ("qrT", "krT") for t in range(NT)]
           + [("pT0", g) for g in range(2)] + [("pT1", g) for g in range(4)]
           + [("yaT", t, g) for t in range(NT) for g in range(2)]
           + [("gate", b, g) for b in range(4) for g in range(2)]
           + [("yrT", t, g) for t in range(NT) for g in range(2)]
           + [("x1T", t, g) for t in range(NT) for g in range(2)])
ND, NA = len(D_FILLS), len(A_FILLS)
assert ND % 4 == 0 and NA % 4 == 0

CONSTS = {}
_at = 0
for _n, _w in (("ident", P), ("alpha_i", P), ("mask", 2 * P), ("decay", RH * SEQ), ("cos_a", NT * MD),
               ("sin_a", NT * MD), ("cos_r", NT * RK), ("sin_r", NT * RK), ("iota", NSEL)):
    CONSTS[_n] = (_at, _w)
    _at += _w
N_CONST = _at


def build(nc, x, w_in, w_moba_out, w_ret_out, w_out, ln1_g, ln1_b, peer_w_query, peer_sub_keys,
          peer_u, peer_v, ln2_g, ln2_b, consts, out):
    ctx = ExitStack()
    with ctx:
        def sb(name, cols, dt=F32):
            return ctx.enter_context(nc.sbuf_tensor(name, [P, cols], dt))

        def sem(name):
            return ctx.enter_context(nc.semaphore(name))

        const_sb = sb("const_sb", N_CONST)
        w_ring = sb("w_ring", W_RING * UNIT)
        arena = sb("arena", 2 * U_RING * D)
        x_sb = sb("x_sb", NT * D)
        xT_sb = sb("xT_sb", KD * SEQ)
        merged_sb = sb("merged_sb", KD * SEQ)
        qk_sb = sb("qk_sb", 4 * 4 * SEQ)
        ya_sb = sb("ya_sb", 4 * SEQ)
        yr_sb = sb("yr_sb", KD * SEQ)
        lnp_sb = sb("lnp_sb", 4 * D)
        t512 = sb("t512", BLK)
        small = sb("small", 512)

        def const(name):
            o, w = CONSTS[name]
            return const_sb[:, o:o + w]

        ident, alpha_i, mask = const("ident"), const("alpha_i"), const("mask")
        decay = const("decay").rearrange("p (h n) -> p h n", h=RH)
        cos_a = const("cos_a").rearrange("p (t c) -> p t c", t=NT)
        sin_a = const("sin_a").rearrange("p (t c) -> p t c", t=NT)
        cos_r = const("cos_r").rearrange("p (t c) -> p t c", t=NT)
        sin_r = const("sin_r").rearrange("p (t c) -> p t c", t=NT)
        iota = const("iota")

        def cut(whole, sizes):
            at, parts = 0, []
            for s in sizes:
                parts.append(whole[:, at:at + s])
                at += s
            assert at <= whole.shape[-1]
            return parts

        va, vr, gr, gT, p0, p1, pT0, pT1 = cut(
            arena, (NT * 512, NT * D, NT * D, 2 * KD * SEQ, MH * P, MH * SEQ, MH * SEQ, MH * P))
        va = va.rearrange("p (t n) -> p t n", t=NT)
        vr = vr.rearrange("p (t n) -> p t n", t=NT)
        gr = gr.rearrange("p (t n) -> p t n", t=NT)
        gT = gT.rearrange("p (k s) -> p k s", s=SEQ)
        ya = p1.rearrange("p (t n) -> p t n", n=2 * BLK)[:, :, 0:BLK]
        p0 = p0.rearrange("p (h k) -> p h k", h=MH)
        p1 = p1.rearrange("p (h k) -> p h k", h=MH)
        pT0 = pT0.rearrange("p (h q) -> p h q", h=MH)
        pT1 = pT1.rearrange("p (h q) -> p h q", h=MH)
        xs = x_sb[:, :].rearrange("p (t n) -> p t n", t=NT)
        xT = xT_sb[:, :].rearrange("p (k s) -> p k s", k=KD)
        mergedT = merged_sb[:, :].rearrange("p (k s) -> p k s", k=KD)
        rot = merged_sb[:, :].rearrange("p (r n) -> p r n", r=4)
        qaT, kaT, qrT, krT = [q.rearrange("p (c s) -> p c s", s=SEQ) for q in cut(qk_sb, (4 * SEQ,) * 4)]
        scores = qk_sb[:, :]
        yaT = ya_sb[:, :].rearrange("p (c s) -> p c s", s=SEQ)
        yrT = yr_sb[:, :].rearrange("p (c s) -> p c s", s=SEQ)
        sc0, sc1 = cut(yr_sb, (RH * SEQ, RH * P))
        sc0 = sc0.rearrange("p (h n) -> p h n", h=RH)
        sc1 = sc1.rearrange("p (h n) -> p h n", h=RH)
        lnp = lnp_sb[:, :].rearrange("p (i n) -> p i n", i=4)
        qT_ring, key_T, diags, cur, cur2 = cut(merged_sb, (2 * SEQ, 2 * NKEY, DIAGS * P, 2 * NKEY, 2 * NKEY))
        qT_ring = qT_ring.rearrange("p (r s) -> p r s", r=2)
        key_T = key_T.rearrange("p (q k) -> p q k", q=2)
        diags = diags.rearrange("p (r s) -> p r s", r=DIAGS)
        cur = cur.rearrange("p (q k) -> p q k", q=2)
        cur2 = cur2.rearrange("p (q k) -> p q k", q=2)
        cand, cand2, onehot = cut(yr_sb, (NSEL * NSEL, NSEL * NSEL, 2 * NSEL * NSEL))
        onehot4 = onehot.rearrange("p (q k a) -> p q k a", q=2, a=NSEL)
        u_rows = arena[:, 0:U_RING * D].rearrange("p (r n) -> p r n", r=U_RING)
        v_rows = arena[:, U_RING * D:].rearrange("p (r n) -> p r n", r=U_RING)
        (negmax, rsum, rinv, stats, mv, nv, ny, nt, lbase, top, tidxf, fs, posf, picked, gexp, gsum, ginv, gh, hd,
         hx, hth, wts) = cut(small, (16, 16, 16, 48, 16, 8, 8, 8, 1, 32, 32, 16, 32, 32, 16, 1, 1, 16, 16, 16, 16, 16))
        stats = stats.rearrange("p (n c) -> p n c", c=6)
        mv = mv.rearrange("p (n c) -> p n c", c=2)
        top = top.rearrange("p (q k) -> p q k", q=2)
        tidxf = tidxf.rearrange("p (q k) -> p q k", q=2)
        posf = posf.rearrange("p (q k) -> p q k", q=2)
        picked = picked.rearrange("p (q k) -> p q k", q=2)
        ints = sb("ints", 144, U32)
        tidx, pos, pos2, idx_next, *idx = cut(ints, (32, 16, 32, 16) + (NSEL,) * IDX_BUFS)
        tidx = tidx.rearrange("p (q k) -> p q k", q=2)
        pos2 = pos2.rearrange("p (q k) -> p q k", q=2)

        banks = ctx.enter_context(nc.psum_tensor("banks", [P, 8, BLK], F32))
        acc = banks[:, 4:6, :]
        x_ps = banks[:, 6:8, :].rearrange("p a n -> p (a n)")

        def d_bank(*name):
            return banks[:, D_FILLS.index(name) % 4, :]

        def a_bank(*name):
            return banks[:, 4 + A_FILLS.index(name) % 4, :]

        const_in = sem("const_in")
        tables_in = sem("tables_in")
        lnp_in = sem("lnp_in")
        w_in_sem = [sem(f"w_arrived{s}") for s in range(W_RING)]
        w_used = sem("w_used")
        d_full, d_used = sem("d_full"), sem("d_used")
        a_full, a_used = sem("a_full"), sem("a_used")
        th_ready = sem("th_ready")
        max_ready = sem("max_ready")
        exp_ready = sem("exp_ready")
        ln1_done = sem("ln1_done")
        ln2_done = sem("ln2_done")
        q_full, q_used = sem("q_full"), sem("q_used")
        s_full, s_used = sem("s_full"), sem("s_used")
        sel_done = sem("sel_done")
        idx_taken = sem("idx_taken")
        idx_moved = sem("idx_moved")
        order = sem("order")
        fexp_done = sem("fexp_done")
        pre_done = sem("pre_done")
        tanh_done = sem("tanh_done")
        wts_done = sem("wts_done")
        diag_done = sem("diag_done")
        u_in = [sem(f"u_arrived{s}") for s in range(U_RING)]
        v_in = [sem(f"v_arrived{s}") for s in range(U_RING)]
        u_used = sem("u_used")
        v_used = sem("v_used")
        acc_free = sem("acc_free")
        out_done = sem("out_done")

        u_flat = peer_u.rearrange("l e d -> (l e) d")
        v_flat = peer_v.rearrange("l e d -> (l e) d")

        def unit(kind, n):
            k = UNITS.index((kind, n))
            tile = w_ring[:, (k % W_RING) * UNIT:(k % W_RING + 1) * UNIT]
            if kind == "moba":
                return tile[:, 0:4 * BLK].rearrange("p (k n) -> p k n", k=4)
            if kind == "keys":
                return tile[:, 0:2 * PK].rearrange("p (q d) -> p q d", q=2)
            return tile.rearrange("p (k n) -> p k n", k=KD)

        def rot_slot(src, t):
            return {"q_a": 0, "k_a": 2, "q_r": 0, "k_r": 2}[src] + t

        def head_of(t, g, c):
            return g + 2 * c if t == 0 else 4 * (g // 2) + g % 2 + 2 * c

        block = ctx.enter_context(nc.Block())

        @block.sync
        def _(sp):
            sp.dma_start(xs, x[0].rearrange("(t p) n -> p t n", p=P)).then_inc(const_in, 16)
            sp.dma_start(ident, consts[:, 0:P]).then_inc(const_in, 16)
            with sp.Fori(0, DEPTH) as l:
                for k, (kind, n) in enumerate(UNITS):
                    cols = slice(n * BLK, (n + 1) * BLK)
                    if kind == "keys":
                        src = peer_sub_keys[l].rearrange("q k d -> k q d")
                    else:
                        w = {"in": w_in, "moba": w_moba_out, "ret": w_ret_out, "out": w_out,
                             "query": peer_w_query}[kind]
                        src = w[l, :, cols].rearrange("(k p) n -> p k n", p=P)
                    sp.wait_ge(w_used, l * len(UNITS) + k + 1)
                    sp.dma_start(unit(kind, n), src).then_inc(w_in_sem[k % W_RING], 16)
            for t in range(NT):
                sp.wait_ge(ln2_done, NT * (DEPTH - 1) + t + 2)
                sp.dma_start(out[0, t * P:(t + 1) * P, :], xs[:, t, :]).then_inc(out_done, 16)
            sp.wait_ge(out_done, 16 * NT)

        @block.gpsimd
        def _(pool):
            def u_gather(i, b, j):
                pool.wait_ge(u_used, i * NSEL + j + 1)
                pool.sem_inc(order, 1)
                pool.indirect_dma_start(u_rows[:, j % U_RING, :], None, u_flat,
                                        bass.IndirectOffsetOnAxis(ap=idx[b][:, j:j + 1], axis=0)
                                        ).then_inc(u_in[j % U_RING], 16)

            def v_gather(i, b, j):
                pool.wait_ge(v_used, i * NSEL + j + 1)
                pool.sem_inc(order, 1)
                pool.indirect_dma_start(v_rows[:, j % U_RING, :], None, v_flat,
                                        bass.IndirectOffsetOnAxis(ap=idx[b][:, j:j + 1], axis=0)
                                        ).then_inc(v_in[j % U_RING], 16)

            def take(i, b):
                pool.wait_ge(sel_done, i + 1)
                pool.sem_inc(order, 1)
                pool.tensor_copy(idx[b], idx_next).then_inc(idx_moved, 1)
                pool.wait_ge(idx_moved, i + 1)
                pool.sem_inc(idx_taken, 1)

            with pool.Fori(0, DEPTH) as l:
                take(l * HEADS, 0)
                for j in range(NSEL):
                    u_gather(l * HEADS, 0, j)
                with pool.Fori(1, HEADS, IDX_BUFS) as h:
                    for step in range(IDX_BUFS):
                        b = (1 + step) % IDX_BUFS
                        i = l * HEADS + h + step
                        take(i, b)
                        for j in range(NSEL):
                            u_gather(i, b, j)
                            v_gather(i - 1, (b - 1) % IDX_BUFS, j)
                for j in range(NSEL):
                    v_gather(l * HEADS + HEADS - 1, (HEADS - 1) % IDX_BUFS, j)

        @block.tensor
        def _(pe):
            pe.sem_inc(w_used, W_RING)
            pe.sem_inc(v_used, U_RING)
            pe.wait_ge(const_in, 32)
            with pe.Fori(0, DEPTH) as l:
                def unit_in(kind, n):
                    k = UNITS.index((kind, n))
                    pe.wait_ge(w_in_sem[k % W_RING], l * (16 * len(UNITS) // W_RING) + 16 * (k // W_RING + 1))
                    return unit(kind, n)

                def d_start(*name):
                    pe.wait_ge(d_used, l * ND + D_FILLS.index(name) + 1)
                    return d_bank(*name)

                def a_start(*name):
                    pe.wait_ge(a_used, l * NA + A_FILLS.index(name) + 1)
                    return a_bank(*name)

                def d_ready(*name):
                    pe.wait_ge(d_used, l * ND + D_FILLS.index(name) + 5)

                def a_ready(*name):
                    pe.wait_ge(a_used, l * NA + A_FILLS.index(name) + 5)

                def transposes(tiles, bank):
                    for c, tile in enumerate(tiles):
                        last = pe.transpose(bank[:, c * P:(c + 1) * P], tile, ident)
                    return last

                pe.wait_ge(ln2_done, l * NT + 1)
                for t in range(NT):
                    for g in range(2):
                        bank = a_start("xT", t, g)
                        transposes([xs[:, t, (4 * g + c) * P:(4 * g + c + 1) * P] for c in range(4)],
                                   bank).then_inc(a_full, 1)
                for t in range(NT):
                    a_ready("xT", t, 1)

                def block_(kind, n, name):
                    w = unit_in("in", n)
                    start, full = (d_start, d_full) if kind == "d" else (a_start, a_full)
                    for t in range(NT):
                        bank = start(name, t)
                        for k in range(KD):
                            last = pe.matmul(bank, xT[:, k, t * P:(t + 1) * P], w[:, k, :],
                                             start=(k == 0), stop=(k == KD - 1))
                        last.then_inc(full, 1)
                    pe.wait_ge(full, fills(full, name))
                    pe.sem_inc(w_used, 1)

                def fills(full, name):
                    if full is d_full:
                        return l * ND + D_FILLS.index((name, NT - 1)) + 1
                    return l * NA + A_FILLS.index((name, NT - 1)) + 1

                def qk_transposes(src, dst):
                    for t in range(NT):
                        d_ready(src, t)
                        bank = a_start(dst, t)
                        r = rot_slot(src, t)
                        transposes([rot[:, r, c * P:(c + 1) * P] for c in range(4)], bank).then_inc(a_full, 1)

                block_("d", 0, "q_a")
                block_("d", 1, "k_a")
                block_("a", 2, "v_a")
                qk_transposes("q_a", "qaT")
                qk_transposes("k_a", "kaT")
                block_("d", 3, "q_r")
                a_ready("kaT", 1)
                for t, per in ((0, 4), (1, 2)):
                    for g in range(MH // per):
                        bank = d_start(f"s{t}", g)
                        keys = (t + 1) * P
                        for c in range(per):
                            h = head_of(t, g, c)
                            rows = slice(MD * (h % 2), MD * (h % 2) + MD)
                            last = pe.matmul(bank[:, c * keys:(c + 1) * keys], qaT[rows, h // 2, t * P:(t + 1) * P],
                                             kaT[rows, h // 2, 0:keys], start=True, stop=True)
                        last.then_inc(d_full, 1)
                block_("d", 4, "k_r")
                block_("a", 5, "v_r0")
                block_("a", 6, "v_r1")
                qk_transposes("q_r", "qrT")
                qk_transposes("k_r", "krT")
                pe.wait_ge(exp_ready, l * NT * MH + MH)
                for g in range(2):
                    bank = a_start("pT0", g)
                    transposes([p0[:, 4 * g + c, :] for c in range(4)], bank).then_inc(a_full, 1)
                pe.wait_ge(exp_ready, l * NT * MH + 2 * MH)
                for g in range(4):
                    bank = a_start("pT1", g)
                    transposes([p1[:, 2 * g + c // 2, (c % 2) * P:(c % 2 + 1) * P] for c in range(4)],
                               bank).then_inc(a_full, 1)
                a_ready("krT", 1)
                for g in range(2):
                    bank = d_start("sc0", g)
                    for c in range(2):
                        h = 2 * g + c
                        last = pe.matmul(bank[:, c * SEQ:(c + 1) * SEQ], krT[:, h, 0:P], qrT[:, h, :],
                                         start=True, stop=True)
                    last.then_inc(d_full, 1)
                for g in range(2):
                    bank = d_start("sc1", g)
                    for c in range(2):
                        h = 2 * g + c
                        last = pe.matmul(bank[:, c * P:(c + 1) * P], krT[:, h, P:SEQ], qrT[:, h, P:SEQ],
                                         start=True, stop=True)
                    last.then_inc(d_full, 1)
                block_("d", 7, "g_r0")
                block_("d", 8, "g_r1")
                a_ready("pT1", 3)
                for t in range(NT):
                    bank = d_start("ya", t)
                    for h in range(MH):
                        o = bank[:, h * MD:(h + 1) * MD]
                        v = slice(h * MD, (h + 1) * MD)
                        last = pe.matmul(o, pT0[:, h, t * P:(t + 1) * P], va[:, 0, v], start=True, stop=(t == 0))
                        if t == 1:
                            last = pe.matmul(o, pT1[:, h, :], va[:, 1, v], start=False, stop=True)
                    last.then_inc(d_full, 1)
                d_ready("sc1", 1)
                for t in range(NT):
                    for g in range(2):
                        bank = d_start("yr", t, g)
                        for c in range(2):
                            h = 2 * g + c
                            o = bank[:, c * RV:(c + 1) * RV]
                            v = slice(h * RV, (h + 1) * RV)
                            last = pe.matmul(o, sc0[:, h, t * P:(t + 1) * P], vr[:, 0, v],
                                             start=True, stop=(t == 0))
                            if t == 1:
                                last = pe.matmul(o, sc1[:, h, :], vr[:, 1, v], start=False, stop=True)
                        last.then_inc(d_full, 1)
                for t in range(NT):
                    d_ready("ya", t)
                    for g in range(2):
                        bank = a_start("yaT", t, g)
                        transposes([ya[:, t, (2 * g + c) * P:(2 * g + c + 1) * P] for c in range(2)],
                                   bank).then_inc(a_full, 1)
                for b in range(4):
                    w = unit_in("in", 9 + b)
                    for g in range(2):
                        bank = a_start("gate", b, g)
                        for c in range(2):
                            col = (2 * g + c) * P
                            for k in range(KD):
                                last = pe.matmul(bank[:, c * SEQ:(c + 1) * SEQ], w[:, k, col:col + P], xT[:, k, :],
                                                 start=(k == 0), stop=(k == KD - 1))
                        last.then_inc(a_full, 1)
                    pe.wait_ge(a_full, l * NA + A_FILLS.index(("gate", b, 1)) + 1)
                    pe.sem_inc(w_used, 1)
                d_ready("yr", 1, 1)
                for t in range(NT):
                    for g in range(2):
                        bank = a_start("yrT", t, g)
                        transposes([gr[:, t, (4 * g + c) * P:(4 * g + c + 1) * P] for c in range(4)],
                                   bank).then_inc(a_full, 1)
                a_ready("yrT", 1, 1)
                for hf in range(2):
                    for which, (kind, y, kk) in enumerate((("moba", yaT, 4), ("ret", yrT, KD))):
                        w = unit_in(kind, hf)
                        for g in range(2):
                            bank = d_start("br", hf, which, g)
                            for c in range(2):
                                col = (2 * g + c) * P
                                for k in range(kk):
                                    last = pe.matmul(bank[:, c * SEQ:(c + 1) * SEQ], w[:, k, col:col + P],
                                                     y[:, k, :], start=(k == 0), stop=(k == kk - 1))
                            last.then_inc(d_full, 1)
                        pe.wait_ge(d_full, l * ND + D_FILLS.index(("br", hf, which, 1)) + 1)
                        pe.sem_inc(w_used, 1)
                d_ready("br", 1, 1, 1)
                w_halves = [unit_in("out", hf) for hf in range(2)]
                for t in range(NT):
                    for hf in range(2):
                        bank = d_start("mix", hf, t)
                        for k in range(KD):
                            last = pe.matmul(bank, mergedT[:, k, t * P:(t + 1) * P], w_halves[hf][:, k, :],
                                             start=(k == 0), stop=(k == KD - 1))
                        last.then_inc(d_full, 1)
                        if t == NT - 1:
                            pe.wait_ge(d_full, l * ND + D_FILLS.index(("mix", hf, t)) + 1)
                            pe.sem_inc(w_used, 1)
                def x1_transposes(t):
                    pe.wait_ge(ln1_done, l * NT + t + 1)
                    for g in range(2):
                        bank = a_start("x1T", t, g)
                        transposes([xs[:, t, (4 * g + c) * P:(4 * g + c + 1) * P] for c in range(4)],
                                   bank).then_inc(a_full, 1)
                    a_ready("x1T", t, 1)

                nq, ns = 2 + len(QUERY_STEPS), len(QUERY_STEPS)
                x1_transposes(0)
                keys = unit_in("keys", 0)
                for q in range(2):
                    pe.wait_ge(q_used, l * nq + q + 1)
                    pe.transpose(banks[:, q, 0:NKEY], keys[:, q, :], ident).then_inc(q_full, 1)
                pe.wait_ge(q_full, l * nq + 2)
                pe.sem_inc(w_used, 1)

                def queries(n):
                    hp, chunks = QUERY_STEPS[n]
                    tok = slice(chunks[0] * P, (chunks[-1] + 1) * P)
                    w = unit_in("query", hp // 4)
                    pe.wait_ge(q_used, l * nq + 2 + n + 1)
                    for k in range(KD):
                        last = pe.matmul(banks[:, n % 2, tok], w[:, k, (hp % 4) * P:(hp % 4 + 1) * P],
                                         xT[:, k, tok], start=(k == 0), stop=(k == KD - 1))
                    last.then_inc(q_full, 1)
                    if hp % 4 == 3 and chunks[-1] == NT - 1:
                        pe.wait_ge(q_full, l * nq + 2 + n + 1)
                        pe.sem_inc(w_used, 1)

                def head_scores(n):
                    hp, chunks = QUERY_STEPS[n]
                    pe.wait_ge(q_used, l * nq + 2 + n + 3)
                    pe.wait_ge(s_used, l * (ns + 2) + n + 1)
                    for c in chunks:
                        last = pe.matmul(banks[:, 2 + n % 2, c * NKEY:(c + 1) * NKEY],
                                         qT_ring[:, n % 2, c * P:(c + 1) * P], key_T[:, hp % 2, :],
                                         start=True, stop=True)
                    last.then_inc(s_full, 1)

                for n, (hp, chunks) in enumerate(QUERY_STEPS):
                    if n == 4:
                        x1_transposes(1)
                    queries(n)
                    if n == 1:
                        d_ready("mix", 1, 1)
                    if n >= 1:
                        head_scores(n - 1)
                head_scores(ns - 1)

                for c in range(NT):
                    pe.wait_ge(acc_free, l * NT + c + 1)
                    for hf in range(2):
                        pe.matmul(acc[:, hf, :], alpha_i, xs[:, c, hf * BLK:(hf + 1) * BLK], start=True, stop=False)

                    def sum_head(i, closes=False):
                        for j in range(NSEL):
                            pe.wait_ge(diag_done, i * NSEL + j + 2)
                            pe.wait_ge(v_in[j % U_RING], i * (16 * NSEL // U_RING) + 16 * (j // U_RING + 1))
                            for hf in range(2):
                                last = pe.matmul(acc[:, hf, :], diags[:, j % DIAGS, :],
                                                 v_rows[:, j % U_RING, hf * BLK:(hf + 1) * BLK],
                                                 start=False, stop=closes and j == NSEL - 1)
                            last.then_inc(v_used, 1)

                    with pe.Fori(c * PH, (c + 1) * PH - 1) as h:
                        sum_head(l * HEADS + h)
                    sum_head(l * HEADS + (c + 1) * PH - 1, closes=True)

        @block.scalar
        def _(act):
            act.sem_inc(a_used, 4)
            act.sem_inc(q_used, 2)
            act.sem_inc(s_used, 2)
            act.sem_inc(fexp_done, 1)
            act.sem_inc(diag_done, 1)
            act.wait_ge(const_in, 32)
            act.dma_start(const_sb[:, P:], consts[:, P:]).then_inc(tables_in, 16)
            with act.Fori(0, DEPTH) as l:
                def a_wait(*name):
                    act.wait_ge(a_full, l * NA + A_FILLS.index(name) + 1)
                    return a_bank(*name)

                def copy(dst, src, sem_):
                    act.activation(dst, src, ACT.Copy).then_inc(sem_, 1)

                def four(bank):
                    return bank.rearrange("p (c s) -> p c s", c=4)

                act.wait_ge(ln2_done, l * NT + 1)
                for n, prm in enumerate((ln1_g, ln1_b, ln2_g, ln2_b)):
                    act.dma_start(lnp[:, n, :], prm[l].partition_broadcast(P)).then_inc(lnp_in, 16)
                for t in range(NT):
                    for g in range(2):
                        copy(xT[:, 4 * g:4 * g + 4, t * P:(t + 1) * P], four(a_wait("xT", t, g)), a_used)
                for t in range(NT):
                    copy(va[:, t, :], a_wait("v_a", t), a_used)
                for dst, name in ((qaT, "qaT"), (kaT, "kaT")):
                    for t in range(NT):
                        copy(dst[:, :, t * P:(t + 1) * P], four(a_wait(name, t)), a_used)
                for t, p in ((0, p0), (1, p1)):
                    act.wait_ge(max_ready, l * NT + t + 1)
                    for h in range(MH):
                        act.activation(p[:, h, :], p[:, h, :], ACT.Exp, bias=negmax[:, t * MH + h:t * MH + h + 1],
                                       accum_out=rsum[:, t * MH + h:t * MH + h + 1]).then_inc(exp_ready, 1)
                for hf in range(2):
                    for t in range(NT):
                        copy(vr[:, t, hf * BLK:(hf + 1) * BLK], a_wait(f"v_r{hf}", t), a_used)
                for dst, name in ((qrT, "qrT"), (krT, "krT")):
                    for t in range(NT):
                        copy(dst[:, :, t * P:(t + 1) * P], four(a_wait(name, t)), a_used)
                for g in range(2):
                    copy(pT0[:, 4 * g:4 * g + 4, 0:P], four(a_wait("pT0", g)), a_used)
                for g in range(4):
                    bank = four(a_wait("pT1", g))
                    act.activation(pT0[:, 2 * g:2 * g + 2, P:SEQ], bank[:, 0::2, :], ACT.Copy)
                    copy(pT1[:, 2 * g:2 * g + 2, :], bank[:, 1::2, :], a_used)
                for hf in range(2):
                    for t in range(NT):
                        act.wait_ge(d_full, l * ND + D_FILLS.index((f"g_r{hf}", t)) + 1)
                        act.activation(gr[:, t, hf * BLK:(hf + 1) * BLK], d_bank(f"g_r{hf}", t), ACT.Tanh,
                                       scale=0.5).then_inc(th_ready, 1)
                for t in range(NT):
                    for g in range(2):
                        copy(yaT[:, 2 * g:2 * g + 2, t * P:(t + 1) * P],
                             four(a_wait("yaT", t, g))[:, 0:2, :], a_used)
                for b in range(4):
                    for g in range(2):
                        bank = a_wait("gate", b, g)
                        act.activation(gT[:, 4 * b + 2 * g:4 * b + 2 * g + 2, :],
                                       bank.rearrange("p (c s) -> p c s", c=2), ACT.Tanh,
                                       scale=0.5).then_inc(a_used, 1)
                def transposed(name, dst, t):
                    for g in range(2):
                        copy(dst[:, 4 * g:4 * g + 4, t * P:(t + 1) * P], four(a_wait(name, t, g)), a_used)

                for t in range(NT):
                    transposed("yrT", yrT, t)

                nq, ns = 2 + len(QUERY_STEPS), len(QUERY_STEPS)
                transposed("x1T", xT, 0)
                for q in range(2):
                    act.wait_ge(q_full, l * nq + q + 1)
                    copy(key_T[:, q, :], banks[:, q, 0:NKEY], q_used)
                by_head = scores.rearrange("p (c h k) -> p c h k", c=NT, k=NKEY)

                def query_out(n):
                    chunks = QUERY_STEPS[n][1]
                    tok = slice(chunks[0] * P, (chunks[-1] + 1) * P)
                    act.wait_ge(q_full, l * nq + 2 + n + 1)
                    if n >= 2:
                        act.wait_ge(s_full, l * ns + n - 1)
                    copy(qT_ring[:, n % 2, tok], banks[:, n % 2, tok], q_used)

                def scores_out(n):
                    hp, chunks = QUERY_STEPS[n]
                    cs = slice(chunks[0], chunks[-1] + 1)
                    act.wait_ge(s_full, l * ns + n + 1)
                    copy(by_head[:, cs, hp, :],
                         banks[:, 2 + n % 2, 0:NT * NKEY].rearrange("p (c k) -> p c k", c=NT)[:, cs, :], s_used)

                def final_exp(i):
                    act.wait_ge(sel_done, i + 1)
                    act.activation(gexp, fs, ACT.Exp, bias=negmax[:, 0:1], accum_out=gsum).then_inc(fexp_done, 1)

                def tanh_of(i):
                    act.wait_ge(pre_done, i + 1)
                    act.activation(hth, hx, ACT.Tanh, scale=GELU_C).then_inc(tanh_done, 1)

                def diagonals(i):
                    for j in range(NSEL):
                        act.wait_ge(v_used, i * NSEL + j + 1 + U_RING - DIAGS)
                        act.activation(diags[:, j % DIAGS, :], ident, ACT.Copy,
                                       scale=wts[:, j:j + 1]).then_inc(diag_done, 1)

                for n in range(ns):
                    if n == 4:
                        transposed("x1T", xT, 1)
                    query_out(n)
                    if n >= 1:
                        scores_out(n - 1)
                    if n == FIRST_EXP:
                        final_exp(l * HEADS)
                scores_out(ns - 1)
                act.drain().then_inc(s_used, 2)
                with act.Fori(0, HEADS - 1) as h:
                    i = l * HEADS + h
                    tanh_of(i)
                    act.wait_ge(wts_done, i + 1)
                    final_exp(i + 1)
                    diagonals(i)
                last = l * HEADS + HEADS - 1
                tanh_of(last)
                act.wait_ge(wts_done, last + 1)
                diagonals(last)

        @block.vector
        def _(dve):
            def settle():
                dve.drain()

            def rsqrt(n, eps, gain):
                v, y, t = nv[:, 0:n], ny[:, 0:n], nt[:, 0:n]
                settle()
                dve.tensor_scalar(v, mv[:, 0:n, 1], eps, None, ALU.add)
                settle()
                dve.tensor_scalar(t.bitcast(I32), v.bitcast(I32), 1, None, ALU.logical_shift_right)
                settle()
                dve.tensor_scalar(y.bitcast(I32), t.bitcast(I32), -1.0, float(0x5F3759DF), ALU.mult, ALU.add)
                settle()
                for step in range(3):
                    dve.tensor_tensor(t, y, y, ALU.mult)
                    settle()
                    dve.tensor_tensor(t, t, v, ALU.mult)
                    settle()
                    g = gain if step == 2 else 1.0
                    dve.tensor_scalar(t, t, -0.5 * g, 1.5 * g, ALU.mult, ALU.add)
                    settle()
                    dve.tensor_tensor(y, y, t, ALU.mult)
                    settle()

            dve.memset(lbase, 0.0)
            dve.sem_inc(d_used, 4)
            dve.sem_inc(ln2_done, 1)
            dve.sem_inc(u_used, U_RING)
            dve.sem_inc(acc_free, 1)
            dve.sem_inc(idx_taken, 1)
            dve.wait_ge(tables_in, 16)
            dve.wait_ge(const_in, 32)
            with dve.Fori(0, DEPTH) as l:
                def d_wait(*name):
                    dve.wait_ge(d_full, l * ND + D_FILLS.index(name) + 1)
                    return d_bank(*name)

                def rope(src, t, heads, view, cos, sin):
                    bank = d_wait(src, t)
                    o = rot[:, rot_slot(src, t), :]
                    n = BLK // heads
                    cosb = cos[:, t, :].unsqueeze(1).to_broadcast([P, heads, n])
                    dve.tensor_tensor(o.rearrange("p (h c) -> p h c", h=heads),
                                      bank.rearrange("p (h c) -> p h c", h=heads), cosb, ALU.mult)
                    s = sin[:, t, :].unsqueeze(1).to_broadcast([P, heads, n])
                    for half in range(2):
                        dve.tensor_tensor(view(t512[:, :].rearrange("p (h c) -> p h c", h=heads), half),
                                          view(bank.rearrange("p (h c) -> p h c", h=heads), 1 - half),
                                          view(s, half), ALU.mult)
                    settle()
                    dve.tensor_tensor(o, o, t512[:, :], ALU.add).then_inc(d_used, 1)
                    settle()

                def halves(a, half):
                    n = a.shape[-1] // 2
                    return a[:, :, half * n:(half + 1) * n]

                def pairs(a, half):
                    return a[:, :, half::2]

                for t in range(NT):
                    rope("q_a", t, MH, halves, cos_a, sin_a)
                for t in range(NT):
                    rope("k_a", t, MH, halves, cos_a, sin_a)
                dve.wait_ge(a_full, l * NA + A_FILLS.index(("qaT", 1)) + 1)
                for t in range(NT):
                    rope("q_r", t, RH, pairs, cos_r, sin_r)
                for t, p, per in ((0, p0, 4), (1, p1, 2)):
                    keys = (t + 1) * P
                    m = mask[:, (1 - t) * P:2 * P].unsqueeze(1).to_broadcast([P, per, keys])
                    for g in range(MH // per):
                        bank = d_wait(f"s{t}", g)
                        first = head_of(t, g, 0)
                        dve.scalar_tensor_tensor(p[:, first:first + 2 * per - 1:2, :],
                                                 bank.rearrange("p (h k) -> p h k", h=per), SCALE, m,
                                                 ALU.mult, ALU.add).then_inc(d_used, 1)
                    settle()
                    dve.tensor_reduce(negmax[:, t * MH:(t + 1) * MH], p, AX_X, ALU.max,
                                      negate=True).then_inc(max_ready, 1)
                dve.wait_ge(a_full, l * NA + A_FILLS.index(("kaT", 1)) + 1)
                for t in range(NT):
                    rope("k_r", t, RH, pairs, cos_r, sin_r)
                for g in range(2):
                    bank = d_wait("sc0", g)
                    dve.tensor_tensor(sc0[:, 2 * g:2 * g + 2, :], bank.rearrange("p (h n) -> p h n", h=2),
                                      decay[:, 2 * g:2 * g + 2, :], ALU.mult).then_inc(d_used, 1)
                for g in range(2):
                    bank = d_wait("sc1", g)
                    dve.tensor_tensor(sc1[:, 2 * g:2 * g + 2, :],
                                      bank[:, 0:2 * P].rearrange("p (h n) -> p h n", h=2),
                                      decay[:, 2 * g:2 * g + 2, 0:P], ALU.mult).then_inc(d_used, 1)
                for hf in range(2):
                    for t in range(NT):
                        o = gr[:, t, hf * BLK:(hf + 1) * BLK]
                        dve.wait_ge(th_ready, l * 2 * NT + hf * NT + t + 1)
                        dve.scalar_tensor_tensor(o, o, 1.0, d_wait(f"g_r{hf}", t), ALU.add,
                                                 ALU.mult).then_inc(d_used, 1)
                dve.reciprocal(rinv, rsum)
                settle()
                for t in range(NT):
                    bank = d_wait("ya", t)
                    r = rinv[:, t * MH:(t + 1) * MH].unsqueeze(2).to_broadcast([P, MH, MD])
                    dve.tensor_tensor(ya[:, t, :].rearrange("p (h c) -> p h c", h=MH),
                                      bank.rearrange("p (h c) -> p h c", h=MH), r, ALU.mult).then_inc(d_used, 1)
                for t in range(NT):
                    for h in range(RH):
                        bank = d_wait("yr", t, h // 2)
                        dve.bn_stats(stats[:, t * RH + h, :], bank[:, (h % 2) * RV:(h % 2 + 1) * RV])
                settle()
                for n in range(NT * RH):
                    dve.bn_aggr(mv[:, n, :], stats[:, n, :])
                rsqrt(NT * RH, EPS, 0.5)
                for t in range(NT):
                    for h in range(RH):
                        n = t * RH + h
                        bank = d_bank("yr", t, h // 2)
                        o = gr[:, t, h * RV:(h + 1) * RV]
                        tmp = t512[:, (h % 2) * RV:(h % 2 + 1) * RV]
                        read = dve.tensor_scalar(tmp, bank[:, (h % 2) * RV:(h % 2 + 1) * RV], mv[:, n, 0:1],
                                                 ny[:, n:n + 1], ALU.subtract, ALU.mult)
                        settle()
                        done = dve.tensor_tensor(o, o, tmp, ALU.mult)
                        if h % 2:
                            done.then_inc(d_used, 1)
                            settle()
                dve.wait_ge(a_used, l * NA + A_FILLS.index(("gate", 3, 1)) + 5)
                dve.wait_ge(a_full, l * NA + A_FILLS.index(("krT", 1)) + 1)
                for hf in range(2):
                    for which in range(2):
                        for g in range(2):
                            c = 4 * hf + 2 * g
                            o = mergedT[:, c:c + 2, :]
                            b = d_wait("br", hf, which, g).rearrange("p (c s) -> p c s", c=2)
                            gate = gT[:, KD * which + c:KD * which + c + 2, :]
                            if which == 0:
                                dve.scalar_tensor_tensor(o, gate, 1.0, b, ALU.add, ALU.mult).then_inc(d_used, 1)
                            else:
                                o2 = t512[:, :].rearrange("p (c s) -> p c s", c=2)
                                dve.scalar_tensor_tensor(o2, gate, 1.0, b, ALU.add, ALU.mult)
                                settle()
                                dve.tensor_tensor(o, o, o2, ALU.add).then_inc(d_used, 1)
                                settle()
                dve.wait_ge(lnp_in, 64 * l + 64)
                for t in range(NT):
                    for hf in range(2):
                        o = xs[:, t, hf * BLK:(hf + 1) * BLK]
                        dve.scalar_tensor_tensor(o, o, 2.0 * ALPHA, d_wait("mix", hf, t), ALU.mult,
                                                 ALU.add).then_inc(d_used, 1)
                        settle()
                        dve.bn_stats(stats[:, hf, :], o)
                    settle()
                    dve.bn_aggr(mv[:, 0, :], stats[:, 0:2, :])
                    rsqrt(1, 4.0 * EPS, 1.0)
                    o = xs[:, t, :]
                    dve.tensor_scalar(o, o, mv[:, 0, 0:1], ny[:, 0:1], ALU.subtract, ALU.mult)
                    settle()
                    dve.tensor_tensor(o, o, lnp[:, 0, :], ALU.mult)
                    settle()
                    dve.tensor_tensor(o, o, lnp[:, 1, :], ALU.add).then_inc(ln1_done, 1)
                settle()

                def select(i, h, fresh=None):
                    if fresh is not None:
                        dve.wait_ge(s_used, l * (len(QUERY_STEPS) + 2) + fresh)
                    dve.tensor_copy(cur.rearrange("p q k -> p (q k)"), scores[:, bass.ds(h * 2 * NKEY, 2 * NKEY)])
                    settle()
                    for q in range(2):
                        dve.max(top[:, q, 0:8], cur[:, q, :])
                    settle()
                    for q in range(2):
                        dve.max_index(tidx[:, q, 0:8], top[:, q, 0:8], cur[:, q, :])
                        dve.match_replace(cur2[:, q, :], top[:, q, 0:8], cur[:, q, :], LOWEST)
                    settle()
                    for q in range(2):
                        dve.max(top[:, q, 8:16], cur2[:, q, :])
                    settle()
                    for q in range(2):
                        dve.max_index(tidx[:, q, 8:16], top[:, q, 8:16], cur2[:, q, :])
                    pair = [P, NSEL, NSEL]
                    dve.tensor_tensor(cand.rearrange("p (a b) -> p a b", a=NSEL),
                                      top[:, 0, :].unsqueeze(2).to_broadcast(pair),
                                      top[:, 1, :].unsqueeze(1).to_broadcast(pair), ALU.add)
                    settle()
                    dve.wait_ge(fexp_done, i + 1)
                    dve.tensor_copy(tidxf, tidx)
                    dve.max(fs[:, 0:8], cand)
                    settle()
                    dve.max_index(pos[:, 0:8], fs[:, 0:8], cand)
                    dve.match_replace(cand2, fs[:, 0:8], cand, LOWEST)
                    settle()
                    dve.max(fs[:, 8:16], cand2)
                    dve.tensor_scalar(negmax[:, 0:1], fs[:, 0:1], -1.0, None, ALU.mult)
                    settle()
                    dve.max_index(pos[:, 8:16], fs[:, 8:16], cand2)
                    settle()
                    dve.tensor_scalar(pos2[:, 0, :], pos, 4, None, ALU.logical_shift_right)
                    dve.tensor_scalar(pos2[:, 1, :], pos, NSEL - 1, None, ALU.bitwise_and)
                    settle()
                    dve.tensor_copy(posf, pos2)
                    settle()
                    for q in range(2):
                        dve.tensor_tensor(onehot4[:, q, :, :], posf[:, q, :].unsqueeze(2).to_broadcast(pair),
                                          iota.unsqueeze(1).to_broadcast(pair), ALU.is_equal)
                    settle()
                    for q in range(2):
                        dve.tensor_tensor(onehot4[:, q, :, :], onehot4[:, q, :, :],
                                          tidxf[:, q, :].unsqueeze(1).to_broadcast(pair), ALU.mult)
                    settle()
                    dve.tensor_reduce(picked, onehot4, AX_X, ALU.add)
                    settle()
                    dve.tensor_scalar(picked[:, 0, :], picked[:, 0, :], float(NKEY), lbase, ALU.mult, ALU.add)
                    settle()
                    dve.wait_ge(idx_taken, i + 1)
                    dve.tensor_tensor(idx_next, picked[:, 0, :], picked[:, 1, :], ALU.add).then_inc(sel_done, 1)

                def dots(i):
                    for j in range(NSEL):
                        dve.wait_ge(u_in[j % U_RING], i * (16 * NSEL // U_RING) + 16 * (j // U_RING + 1))
                        row = u_rows[:, j % U_RING, :]
                        dve.tensor_tensor_reduce(out=row, in0=row, in1=x_ps, scale=1.0, scalar=0.0, op0=ALU.mult,
                                                 op1=ALU.add, accum_out=hd[:, j:j + 1]).then_inc(u_used, 1)
                    settle()

                def weights(i):
                    dve.tensor_tensor(hx, hd, hd, ALU.mult)
                    dve.wait_ge(fexp_done, i + 2)
                    dve.reciprocal(ginv, gsum)
                    settle()
                    dve.tensor_scalar(hx, hx, GELU_A, 1.0, ALU.mult, ALU.add)
                    dve.tensor_scalar(gh, gexp, ginv, 0.5, ALU.mult, ALU.mult)
                    settle()
                    dve.tensor_tensor(hx, hx, hd, ALU.mult).then_inc(pre_done, 1)
                    dve.tensor_tensor(gh, gh, hd, ALU.mult)
                    settle()
                    dve.wait_ge(tanh_done, i + 1)
                    dve.wait_ge(diag_done, i * NSEL + 1)
                    dve.scalar_tensor_tensor(wts, hth, 1.0, gh, ALU.add, ALU.mult).then_inc(wts_done, 1)

                def dot_operand(c):
                    dve.tensor_copy(x_ps, xs[:, c, :])
                    settle()

                def second_norm(c):
                    dve.wait_ge(v_used, (l * HEADS + (c + 1) * PH) * NSEL + U_RING)
                    for hf in range(2):
                        dve.bn_stats(stats[:, hf, :], acc[:, hf, :])
                    settle()
                    dve.bn_aggr(mv[:, 0, :], stats[:, 0:2, :])
                    rsqrt(1, EPS, 1.0)
                    o = xs[:, c, :]
                    dve.tensor_scalar(o, acc.rearrange("p a n -> p (a n)"), mv[:, 0, 0:1], ny[:, 0:1],
                                      ALU.subtract, ALU.mult).then_inc(acc_free, 1)
                    settle()
                    dve.tensor_tensor(o, o, lnp[:, 2, :], ALU.mult)
                    settle()
                    dve.tensor_tensor(o, o, lnp[:, 3, :], ALU.add).then_inc(ln2_done, 1)

                base = l * HEADS
                select(base, 0, fresh=4)
                dve.wait_ge(a_used, l * NA + NA + 4)
                dot_operand(0)
                select(base + 1, 1, fresh=6)
                dots(base)
                weights(base)
                with dve.Fori(1, PH) as h:
                    select(base + h + 1, h + 1, fresh=2 * h + 10)
                    dots(base + h)
                    weights(base + h)
                dot_operand(1)
                select(base + PH + 1, PH + 1)
                dots(base + PH)
                weights(base + PH)
                second_norm(0)
                with dve.Fori(PH + 1, HEADS - 1) as h:
                    select(base + h + 1, h + 1)
                    dots(base + h)
                    weights(base + h)
                dots(base + HEADS - 1)
                weights(base + HEADS - 1)
                second_norm(1)
                dve.tensor_scalar(lbase, lbase, float(NEXP), None, ALU.add)
                settle()


def shape_constants():
    import numpy as np
    f = np.float32
    c = np.zeros((P, N_CONST), f)

    def put(name, a):
        o, w = CONSTS[name]
        c[:, o:o + w] = np.asarray(a).reshape(P, w)

    put("ident", np.eye(P))
    put("alpha_i", ALPHA * np.eye(P))
    q, k = np.arange(P)[:, None], np.arange(P)[None, :]
    put("mask", np.concatenate([np.zeros((P, P)), np.where(k <= q, 0.0, -1e30)], 1))
    log_g = np.log(1.0 - 2.0 ** (-5.0 - np.arange(RH)))
    diff = np.arange(SEQ)[None, None, :] - np.arange(P)[:, None, None]
    put("decay", np.where(diff >= 0, np.exp(log_g[None, :, None] * np.maximum(diff, 0)), 0.0) * RK ** -0.5)
    pos = (np.arange(NT)[None, :, None] * P + np.arange(P)[:, None, None]).astype(f)
    ang = pos * (f(10000.0) ** (-np.arange(0, MD, 2, dtype=f) / f(MD)))
    put("cos_a", np.concatenate([np.cos(ang), np.cos(ang)], -1))
    put("sin_a", np.concatenate([-np.sin(ang), np.sin(ang)], -1))
    ang = pos * (f(1.0) / f(10000.0) ** np.linspace(0.0, 1.0, RK // 2, dtype=f))
    put("cos_r", np.repeat(np.cos(ang), 2, -1))
    put("sin_r", np.stack([-np.sin(ang), np.sin(ang)], -1))
    put("iota", np.broadcast_to(np.arange(NSEL), (P, NSEL)))
    return c


def kernel(**inputs):
    import numpy as np
    import concourse.bacc as bacc
    from concourse.bass_utils import run_bass_kernel_spmd as run

    names = ["x", "w_in", "w_moba_out", "w_ret_out", "w_out", "ln1_g", "ln1_b", "peer_w_query", "peer_sub_keys",
             "peer_u", "peer_v", "ln2_g", "ln2_b"]
    nc = bacc.Bacc("TRN2", target_bir_lowering=False, num_devices=1)
    arrays = {f"in_{n}": np.ascontiguousarray(inputs[n]) for n in names}
    arrays["in_consts"] = shape_constants()
    args = [nc.dram_tensor(n, a.shape, mybir.dt.from_np(a.dtype), kind="ExternalInput").ap()
            for n, a in arrays.items()]
    out = nc.dram_tensor("out", (1, SEQ, D), F32, kind="ExternalOutput").ap()
    build(nc, *args, out)
    return run(nc, [arrays], core_ids=[0]).results[0]["out"]
```

```python
from contextlib import ExitStack

import concourse.bass as bass
from concourse import mybir

F32 = mybir.dt.float32
R32 = mybir.dt.float32r
I32 = mybir.dt.int32
U32 = mybir.dt.uint32
ALU = mybir.AluOpType
ACT = mybir.ActivationFunctionType
AX_X = mybir.AxisListType.X

P = 128
D = 1024
KD = D // P
SEQ = 256
NT = SEQ // P
DEPTH = 2
IN_WIDTH = 6656
BLK = 512
MH, MD = 8, 64
RH, RK, RV = 4, 128, 256
PH, PK, NKEY, NSEL = 8, 128, 128, 16
NEXP = NKEY * NKEY
ALPHA = (2.0 * DEPTH) ** 0.25
EPS = 1e-5
SCALE = MD ** -0.5
GELU_C = 0.7978845608028654
GELU_A = 0.044715
LOWEST = -3.0e38
HEADS = NT * PH

UNITS = ([("in", n) for n in range(IN_WIDTH // BLK)]
         + [("moba", 0), ("ret", 0), ("ret", 1)]
         + [("query", n) for n in range(4)])
N_IN = IN_WIDTH // BLK
W_RING = 2
UNIT = KD * BLK
SPLIT = [k for k, (kind, _) in enumerate(UNITS) if kind in ("in", "ret")]
QUARTERS = 4
GRANULE = UNIT // QUARTERS
G_RING = 3
N_GRAN = len(SPLIT) * QUARTERS
FIRST_GATE = 9
N_WHOLE = len(UNITS) - len(SPLIT)
assert len(UNITS) % W_RING == 0
W_TURN = 16 * len(UNITS) // W_RING
U_RING = 8
DIAGS = 4
QUERY_STEPS = ([(hp, (0,)) for hp in range(4)] + [(hp, (1,)) for hp in range(4)]
               + [(hp, (0, 1)) for hp in range(4, 2 * PH)])
FIRST_EXP = 7
IDX_BUFS = 3
assert (HEADS - 1) % IDX_BUFS == 0

D_FILLS = ([(b, t) for b in ("q_a", "k_a", "q_r") for t in range(NT)]
           + [("s0", g) for g in range(2)] + [("s1", g) for g in range(4)]
           + [("k_r", t) for t in range(NT)]
           + [("sc0", g) for g in range(2)] + [("sc1", g) for g in range(2)]
           + [(b, t) for b in ("g_r0", "g_r1") for t in range(NT)]
           + [("ya", t) for t in range(NT)]
           + [("yr", t, g) for t in range(NT) for g in range(2)]
           + [("br", w, hf, g) for w in range(2) for hf in range(2) for g in range(2)]
           + [("mix", hf, t) for t in range(NT) for hf in range(2)])
A_FILLS = ([("xT", t, g) for t in range(NT) for g in range(2)]
           + [("v_a", t) for t in range(NT)]
           + [(b, t) for b in ("qaT", "kaT") for t in range(NT)]
           + [(b, t) for b in ("v_r0", "v_r1") for t in range(NT)]
           + [(b, t) for b in ("qrT", "krT") for t in range(NT)]
           + [("pT0", g) for g in range(2)] + [("pT1", g) for g in range(4)]
           + [("yaT", t, g) for t in range(NT) for g in range(2)]
           + [("gate", b, g) for b in range(4) for g in range(2)]
           + [("yrT", t, g) for t in range(NT) for g in range(2)]
           + [("x1T", t, g) for t in range(NT) for g in range(2)])
IN_BLOCKS = (("d", "q_a"), ("d", "k_a"), ("a", "v_a"), ("d", "q_r"), ("d", "k_r"), ("a", "v_r0"), ("a", "v_r1"),
             ("d", "g_r0"), ("d", "g_r1"))


def granule_end(n):
    r, q = divmod(n, QUARTERS)
    if r >= FIRST_GATE:
        if q % 2 == 0:
            return "g", 3 * FIRST_GATE + 2 * (r - FIRST_GATE) + q // 2 + 1
        if r < N_IN:
            return "a", A_FILLS.index(("gate", r - FIRST_GATE, q // 2)) + 1
        return "d", D_FILLS.index(("br", 1, r - N_IN, q // 2)) + 1
    if q < QUARTERS - 1:
        return "g", 3 * r + q + 1
    kind, name = IN_BLOCKS[r]
    return kind, (D_FILLS if kind == "d" else A_FILLS).index((name, NT - 1)) + 1


N_G_USED = 3 * FIRST_GATE + 2 * (len(SPLIT) - FIRST_GATE)
ND, NA = len(D_FILLS), len(A_FILLS)
assert ND % 4 == 0 and NA % 4 == 0

CONSTS = {}
_at = 0
for _n, _w in (("ident", P), ("alpha_i", P), ("mask", 2 * P), ("decay", RH * SEQ), ("cos_a", NT * MD),
               ("sin_a", NT * MD), ("cos_r", NT * RK), ("sin_r", NT * RK), ("iota", NSEL)):
    CONSTS[_n] = (_at, _w)
    _at += _w
N_CONST = _at


def build(nc, x, w_in, w_moba_out, w_ret_out, w_out, ln1_g, ln1_b, peer_w_query, peer_sub_keys,
          peer_u, peer_v, ln2_g, ln2_b, consts, out):
    ctx = ExitStack()
    with ctx:
        def sb(name, cols, dt=F32):
            return ctx.enter_context(nc.sbuf_tensor(name, [P, cols], dt))

        def sem(name):
            return ctx.enter_context(nc.semaphore(name))

        const_sb = sb("const_sb", N_CONST)
        w_ring = sb("w_ring", W_RING * UNIT)
        arena = sb("arena", 2 * U_RING * D)
        x_sb = sb("x_sb", NT * D)
        merged_sb = sb("merged_sb", KD * SEQ)
        x_hi = sb("x_hi", KD * SEQ, R32)
        x_lo = sb("x_lo", KD * SEQ, R32)
        g_hi = sb("g_hi", G_RING * GRANULE, R32)
        g_lo = sb("g_lo", G_RING * GRANULE, R32)
        qk_sb = sb("qk_sb", 4 * 4 * SEQ)
        y_sb = sb("y_sb", (4 + KD) * SEQ)
        lnp_sb = sb("lnp_sb", 2 * D)
        t512 = sb("t512", BLK)
        keys_sb = sb("keys_sb", 2 * PK)
        small = sb("small", 512)

        def const(name):
            o, w = CONSTS[name]
            return const_sb[:, o:o + w]

        ident, alpha_i, mask = const("ident"), const("alpha_i"), const("mask")
        decay = const("decay").rearrange("p (h n) -> p h n", h=RH)
        cos_a = const("cos_a").rearrange("p (t c) -> p t c", t=NT)
        sin_a = const("sin_a").rearrange("p (t c) -> p t c", t=NT)
        cos_r = const("cos_r").rearrange("p (t c) -> p t c", t=NT)
        sin_r = const("sin_r").rearrange("p (t c) -> p t c", t=NT)
        iota = const("iota")

        def cut(whole, sizes):
            at, parts = 0, []
            for s in sizes:
                parts.append(whole[:, at:at + s])
                at += s
            assert at <= whole.shape[-1]
            return parts

        gr, gT, va, vr, p0, p1, pT0, pT1 = cut(
            arena, (NT * D, 2 * KD * SEQ, NT * 512, NT * D, MH * P, MH * SEQ, MH * SEQ, MH * P))
        wo = [h.rearrange("p (k n) -> p k n", k=KD)
              for h in cut(arena, (NT * D + 2 * KD * SEQ, UNIT, UNIT))[1:]]
        va = va.rearrange("p (t n) -> p t n", t=NT)
        vr = vr.rearrange("p (t n) -> p t n", t=NT)
        gr = gr.rearrange("p (t n) -> p t n", t=NT)
        gT = gT.rearrange("p (k s) -> p k s", s=SEQ)
        ya = p1.rearrange("p (t n) -> p t n", n=2 * BLK)[:, :, 0:BLK]
        p0 = p0.rearrange("p (h k) -> p h k", h=MH)
        p1 = p1.rearrange("p (h k) -> p h k", h=MH)
        pT0 = pT0.rearrange("p (h q) -> p h q", h=MH)
        pT1 = pT1.rearrange("p (h q) -> p h q", h=MH)
        xs = x_sb[:, :].rearrange("p (t n) -> p t n", t=NT)
        xT = merged_sb[:, :].rearrange("p (k s) -> p k s", k=KD)
        xh = x_hi[:, :].rearrange("p (k s) -> p k s", k=KD)
        xl = x_lo[:, :].rearrange("p (k s) -> p k s", k=KD)
        mergedT = merged_sb[:, :].rearrange("p (k s) -> p k s", k=KD)
        rot = merged_sb[:, :].rearrange("p (r n) -> p r n", r=4)
        qaT, kaT, qrT, krT = [q.rearrange("p (c s) -> p c s", s=SEQ) for q in cut(qk_sb, (4 * SEQ,) * 4)]
        scores = qk_sb[:, :]
        yaT = y_sb[:, 0:4 * SEQ].rearrange("p (c s) -> p c s", s=SEQ)
        yrT = y_sb[:, 4 * SEQ:].rearrange("p (c s) -> p c s", s=SEQ)
        _, sc0, sc1 = cut(y_sb, (4 * SEQ, RH * SEQ, RH * P))
        sc0 = sc0.rearrange("p (h n) -> p h n", h=RH)
        sc1 = sc1.rearrange("p (h n) -> p h n", h=RH)
        lnp = lnp_sb[:, :].rearrange("p (i n) -> p i n", i=2)
        qT_ring, key_T, diags, cur, cur2, cand, cand2, onehot = cut(
            y_sb, (2 * SEQ, 2 * NKEY, DIAGS * P, 2 * NKEY, 2 * NKEY, NSEL * NSEL, NSEL * NSEL, 2 * NSEL * NSEL))
        qT_ring = qT_ring.rearrange("p (r s) -> p r s", r=2)
        key_T = key_T.rearrange("p (q k) -> p q k", q=2)
        diags = diags.rearrange("p (r s) -> p r s", r=DIAGS)
        cur = cur.rearrange("p (q k) -> p q k", q=2)
        cur2 = cur2.rearrange("p (q k) -> p q k", q=2)
        onehot4 = onehot.rearrange("p (q k a) -> p q k a", q=2, a=NSEL)
        u_rows = arena[:, 0:U_RING * D].rearrange("p (r n) -> p r n", r=U_RING)
        v_rows = arena[:, U_RING * D:].rearrange("p (r n) -> p r n", r=U_RING)
        (negmax, rsum, rinv, stats, mv, nv, ny, nt, lbase, top, tidxf, fs, posf, picked, gexp, gsum, ginv, gh, hd,
         hx, hth, wts) = cut(small, (16, 16, 16, 48, 16, 8, 8, 8, 1, 32, 32, 16, 32, 32, 16, 1, 1, 16, 16, 16, 16, 16))
        stats = stats.rearrange("p (n c) -> p n c", c=6)
        mv = mv.rearrange("p (n c) -> p n c", c=2)
        top = top.rearrange("p (q k) -> p q k", q=2)
        tidxf = tidxf.rearrange("p (q k) -> p q k", q=2)
        posf = posf.rearrange("p (q k) -> p q k", q=2)
        picked = picked.rearrange("p (q k) -> p q k", q=2)
        ints = sb("ints", 144, U32)
        tidx, pos, pos2, idx_next, *idx = cut(ints, (32, 16, 32, 16) + (NSEL,) * IDX_BUFS)
        tidx = tidx.rearrange("p (q k) -> p q k", q=2)
        pos2 = pos2.rearrange("p (q k) -> p q k", q=2)

        banks = ctx.enter_context(nc.psum_tensor("banks", [P, 8, BLK], F32))
        acc = banks[:, 4:6, :]
        x_ps = banks[:, 6:8, :].rearrange("p a n -> p (a n)")

        def d_bank(*name):
            return banks[:, D_FILLS.index(name) % 4, :]

        def a_bank(*name):
            return banks[:, 4 + A_FILLS.index(name) % 4, :]

        const_in = sem("const_in")
        tables_in = sem("tables_in")
        lnp_in = sem("lnp_in")
        w_in_sem = [sem(f"w_arrived{s}") for s in range(W_RING)]
        keys_in = sem("keys_in")
        wo_in = [sem(f"w_out_arrived{hf}") for hf in range(2)]
        w_used = sem("w_used")
        xl_done = sem("xl_done")
        hi_done = sem("hi_done")
        lo_done = sem("lo_done")
        g_used = sem("g_used")
        d_full, d_used = sem("d_full"), sem("d_used")
        a_full, a_used = sem("a_full"), sem("a_used")
        th_ready = sem("th_ready")
        max_ready = sem("max_ready")
        exp_ready = sem("exp_ready")
        ln1_done = sem("ln1_done")
        ln2_done = sem("ln2_done")
        q_full, q_used = sem("q_full"), sem("q_used")
        s_full, s_used = sem("s_full"), sem("s_used")
        sel_done = sem("sel_done")
        idx_taken = sem("idx_taken")
        idx_moved = sem("idx_moved")
        order = sem("order")
        fexp_done = sem("fexp_done")
        pre_done = sem("pre_done")
        tanh_done = sem("tanh_done")
        wts_done = sem("wts_done")
        diag_done = sem("diag_done")
        u_in = [sem(f"u_arrived{s}") for s in range(U_RING)]
        v_in = [sem(f"v_arrived{s}") for s in range(U_RING)]
        u_used = sem("u_used")
        v_used = sem("v_used")
        acc_free = sem("acc_free")
        out_done = sem("out_done")

        u_flat = peer_u.rearrange("l e d -> (l e) d")
        v_flat = peer_v.rearrange("l e d -> (l e) d")

        def unit(kind, n):
            k = UNITS.index((kind, n))
            tile = w_ring[:, (k % W_RING) * UNIT:(k % W_RING + 1) * UNIT]
            if kind == "moba":
                return tile.rearrange("p (k n) -> p k n", k=4)
            return tile.rearrange("p (k n) -> p k n", k=KD)

        def granule(n):
            (r, q), slot = divmod(n, QUARTERS), n % G_RING
            w = unit(*UNITS[SPLIT[r]])
            if r < FIRST_GATE:
                part, inner = w[:, 2 * q:2 * q + 2, :], BLK
            else:
                part, inner = w[:, :, q * P:(q + 1) * P], P
            hi, lo = (g[:, slot * GRANULE:(slot + 1) * GRANULE].rearrange("p (k n) -> p k n", n=inner)
                      for g in (g_hi, g_lo))
            return part, hi, lo

        def rot_slot(src, t):
            return {"q_a": 0, "k_a": 2, "q_r": 0, "k_r": 2}[src] + t

        def head_of(t, g, c):
            return g + 2 * c if t == 0 else 4 * (g // 2) + g % 2 + 2 * c

        block = ctx.enter_context(nc.Block())

        @block.sync
        def _(sp):
            sp.dma_start(xs, x[0].rearrange("(t p) n -> p t n", p=P)).then_inc(const_in, 16)
            sp.dma_start(ident, consts[:, 0:P]).then_inc(const_in, 16)
            with sp.Fori(0, DEPTH) as l:
                sp.wait_ge(v_used, l * HEADS * NSEL + 1)
                for k, (kind, n) in enumerate(UNITS):
                    w = {"in": w_in, "moba": w_moba_out, "ret": w_ret_out, "query": peer_w_query}[kind]
                    cols = slice(0, D) if kind == "moba" else slice(n * BLK, (n + 1) * BLK)
                    src = w[l, :, cols].rearrange("(k p) n -> p k n", p=P)
                    before = k - W_RING
                    if before in SPLIT:
                        sp.wait_ge(lo_done, l * N_GRAN + QUARTERS * (SPLIT.index(before) + 1))
                    else:
                        whole = before + 1 - (sum(split <= before for split in SPLIT) if before >= 0 else 0)
                        sp.wait_ge(w_used, l * N_WHOLE + N_WHOLE + whole)
                    sp.dma_start(unit(kind, n), src).then_inc(w_in_sem[k % W_RING], 16)
                    if k == N_IN:
                        sp.dma_start(keys_sb[:, :].rearrange("p (q d) -> p q d", q=2),
                                     peer_sub_keys[l].rearrange("q k d -> k q d")).then_inc(keys_in, 16)
                    hf = k - (N_IN - 2)
                    if hf in (0, 1):
                        sp.wait_ge(a_full, l * NA + A_FILLS.index(("yaT", 1, 1)) + 1)
                        src = w_out[l, :, hf * BLK:(hf + 1) * BLK].rearrange("(k p) n -> p k n", p=P)
                        sp.dma_start(wo[hf], src).then_inc(wo_in[hf], 16)
            for t in range(NT):
                sp.wait_ge(ln2_done, NT * (DEPTH - 1) + t + 2)
                sp.dma_start(out[0, t * P:(t + 1) * P, :], xs[:, t, :]).then_inc(out_done, 16)
            sp.wait_ge(out_done, 16 * NT)

        @block.gpsimd
        def _(pool):
            def u_gather(i, b, j):
                pool.wait_ge(u_used, i * NSEL + j + 1)
                pool.sem_inc(order, 1)
                pool.indirect_dma_start(u_rows[:, j % U_RING, :], None, u_flat,
                                        bass.IndirectOffsetOnAxis(ap=idx[b][:, j:j + 1], axis=0)
                                        ).then_inc(u_in[j % U_RING], 16)

            def v_gather(i, b, j):
                pool.wait_ge(v_used, i * NSEL + j + 1)
                pool.sem_inc(order, 1)
                pool.indirect_dma_start(v_rows[:, j % U_RING, :], None, v_flat,
                                        bass.IndirectOffsetOnAxis(ap=idx[b][:, j:j + 1], axis=0)
                                        ).then_inc(v_in[j % U_RING], 16)

            def take(i, b):
                pool.wait_ge(sel_done, i + 1)
                pool.sem_inc(order, 1)
                pool.tensor_copy(idx[b], idx_next).then_inc(idx_moved, 1)
                pool.wait_ge(idx_moved, i + 1)
                pool.sem_inc(idx_taken, 1)

            with pool.Fori(0, DEPTH) as l:
                for n in range(N_GRAN):
                    w, hi, lo = granule(n)
                    pool.wait_ge(hi_done, l * N_GRAN + n + 1)
                    pool.sem_inc(order, 1)
                    pool.tensor_tensor(lo, w, hi.bitcast(F32), ALU.subtract).then_inc(lo_done, 1)
                take(l * HEADS, 0)
                for j in range(NSEL):
                    u_gather(l * HEADS, 0, j)
                with pool.Fori(1, HEADS, IDX_BUFS) as h:
                    for step in range(IDX_BUFS):
                        b = (1 + step) % IDX_BUFS
                        i = l * HEADS + h + step
                        take(i, b)
                        for j in range(NSEL):
                            u_gather(i, b, j)
                            v_gather(i - 1, (b - 1) % IDX_BUFS, j)
                for j in range(NSEL):
                    v_gather(l * HEADS + HEADS - 1, (HEADS - 1) % IDX_BUFS, j)

        @block.tensor
        def _(pe):
            pe.sem_inc(w_used, N_WHOLE)
            pe.sem_inc(v_used, U_RING)
            pe.wait_ge(const_in, 32)
            with pe.Fori(0, DEPTH) as l:
                def unit_in(kind, n):
                    k = UNITS.index((kind, n))
                    pe.wait_ge(w_in_sem[k % W_RING], l * W_TURN + 16 * (k // W_RING + 1))
                    return unit(kind, n)

                def d_start(*name):
                    pe.wait_ge(d_used, l * ND + D_FILLS.index(name) + 1)
                    return d_bank(*name)

                def a_start(*name):
                    pe.wait_ge(a_used, l * NA + A_FILLS.index(name) + 1)
                    return a_bank(*name)

                def d_ready(*name):
                    pe.wait_ge(d_used, l * ND + D_FILLS.index(name) + 5)

                def a_ready(*name):
                    pe.wait_ge(a_used, l * NA + A_FILLS.index(name) + 5)

                def transposes(tiles, bank):
                    for c, tile in enumerate(tiles):
                        last = pe.transpose(bank[:, c * P:(c + 1) * P], tile, ident)
                    return last

                pe.wait_ge(ln2_done, l * NT + 1)
                for t in range(NT):
                    for g in range(2):
                        bank = a_start("xT", t, g)
                        transposes([xs[:, t, (4 * g + c) * P:(4 * g + c + 1) * P] for c in range(4)],
                                   bank).then_inc(a_full, 1)
                pe.wait_ge(xl_done, l * 4 * NT + 2 * NT)

                def split_product(bank, x_part, w_part, first, last):
                    for n, (a, b) in enumerate(((0, 0), (0, 1), (1, 0))):
                        mm = pe.matmul(bank, x_part[a], w_part[b], start=first and n == 0, stop=last and n == 2)
                    return mm

                def block_(kind, n, name):
                    start, full = (d_start, d_full) if kind == "d" else (a_start, a_full)
                    bank = [start(name, t) for t in range(NT)]
                    for q in range(QUARTERS):
                        _, hi, lo = granule(QUARTERS * n + q)
                        pe.wait_ge(lo_done, l * N_GRAN + QUARTERS * n + q + 1)
                        for t in range(NT):
                            tok = slice(t * P, (t + 1) * P)
                            for kk in range(2):
                                k = 2 * q + kk
                                last = split_product(bank[t], (xh[:, k, tok], xl[:, k, tok]), (hi[:, kk, :], lo[:, kk, :]),
                                                     k == 0, k == KD - 1)
                            if q == QUARTERS - 1:
                                last.then_inc(full, 1)
                        if q < QUARTERS - 1:
                            last.then_inc(g_used, 1)

                def qk_transposes(src, dst):
                    for t in range(NT):
                        d_ready(src, t)
                        bank = a_start(dst, t)
                        r = rot_slot(src, t)
                        transposes([rot[:, r, c * P:(c + 1) * P] for c in range(4)], bank).then_inc(a_full, 1)

                block_("d", 0, "q_a")
                block_("d", 1, "k_a")
                block_("a", 2, "v_a")
                qk_transposes("q_a", "qaT")
                qk_transposes("k_a", "kaT")
                block_("d", 3, "q_r")
                a_ready("kaT", 1)
                for t, per in ((0, 4), (1, 2)):
                    for g in range(MH // per):
                        bank = d_start(f"s{t}", g)
                        keys = (t + 1) * P
                        for c in range(per):
                            h = head_of(t, g, c)
                            rows = slice(MD * (h % 2), MD * (h % 2) + MD)
                            last = pe.matmul(bank[:, c * keys:(c + 1) * keys], qaT[rows, h // 2, t * P:(t + 1) * P],
                                             kaT[rows, h // 2, 0:keys], start=True, stop=True)
                        last.then_inc(d_full, 1)
                block_("d", 4, "k_r")
                block_("a", 5, "v_r0")
                block_("a", 6, "v_r1")
                qk_transposes("q_r", "qrT")
                qk_transposes("k_r", "krT")
                pe.wait_ge(exp_ready, l * NT * MH + MH)
                for g in range(2):
                    bank = a_start("pT0", g)
                    transposes([p0[:, 4 * g + c, :] for c in range(4)], bank).then_inc(a_full, 1)
                pe.wait_ge(exp_ready, l * NT * MH + 2 * MH)
                for g in range(4):
                    bank = a_start("pT1", g)
                    transposes([p1[:, 2 * g + c // 2, (c % 2) * P:(c % 2 + 1) * P] for c in range(4)],
                               bank).then_inc(a_full, 1)
                a_ready("krT", 1)
                for g in range(2):
                    bank = d_start("sc0", g)
                    for c in range(2):
                        h = 2 * g + c
                        last = pe.matmul(bank[:, c * SEQ:(c + 1) * SEQ], krT[:, h, 0:P], qrT[:, h, :],
                                         start=True, stop=True)
                    last.then_inc(d_full, 1)
                for g in range(2):
                    bank = d_start("sc1", g)
                    for c in range(2):
                        h = 2 * g + c
                        last = pe.matmul(bank[:, c * P:(c + 1) * P], krT[:, h, P:SEQ], qrT[:, h, P:SEQ],
                                         start=True, stop=True)
                    last.then_inc(d_full, 1)
                block_("d", 7, "g_r0")
                block_("d", 8, "g_r1")
                a_ready("pT1", 3)
                for t in range(NT):
                    bank = d_start("ya", t)
                    for h in range(MH):
                        o = bank[:, h * MD:(h + 1) * MD]
                        v = slice(h * MD, (h + 1) * MD)
                        last = pe.matmul(o, pT0[:, h, t * P:(t + 1) * P], va[:, 0, v], start=True, stop=(t == 0))
                        if t == 1:
                            last = pe.matmul(o, pT1[:, h, :], va[:, 1, v], start=False, stop=True)
                    last.then_inc(d_full, 1)
                d_ready("sc1", 1)
                for t in range(NT):
                    for g in range(2):
                        bank = d_start("yr", t, g)
                        for c in range(2):
                            h = 2 * g + c
                            o = bank[:, c * RV:(c + 1) * RV]
                            v = slice(h * RV, (h + 1) * RV)
                            last = pe.matmul(o, sc0[:, h, t * P:(t + 1) * P], vr[:, 0, v],
                                             start=True, stop=(t == 0))
                            if t == 1:
                                last = pe.matmul(o, sc1[:, h, :], vr[:, 1, v], start=False, stop=True)
                        last.then_inc(d_full, 1)
                for t in range(NT):
                    d_ready("ya", t)
                    for g in range(2):
                        bank = a_start("yaT", t, g)
                        transposes([ya[:, t, (2 * g + c) * P:(2 * g + c + 1) * P] for c in range(2)],
                                   bank).then_inc(a_full, 1)
                for b in range(4):
                    for c in range(QUARTERS):
                        n = QUARTERS * (FIRST_GATE + b) + c
                        _, hi, lo = granule(n)
                        if c % 2 == 0:
                            bank = a_start("gate", b, c // 2)
                        pe.wait_ge(lo_done, l * N_GRAN + n + 1)
                        o = bank[:, (c % 2) * SEQ:(c % 2 + 1) * SEQ]
                        for k in range(KD):
                            last = split_product(o, (hi[:, k, :], lo[:, k, :]), (xh[:, k, :], xl[:, k, :]),
                                                 k == 0, k == KD - 1)
                        last.then_inc(a_full if c % 2 else g_used, 1)
                d_ready("yr", 1, 1)
                for t in range(NT):
                    for g in range(2):
                        bank = a_start("yrT", t, g)
                        transposes([gr[:, t, (4 * g + c) * P:(4 * g + c + 1) * P] for c in range(4)],
                                   bank).then_inc(a_full, 1)
                a_ready("yaT", 1, 1)
                w = unit_in("moba", 0)
                for hf in range(2):
                    for g in range(2):
                        bank = d_start("br", 0, hf, g)
                        for c in range(2):
                            col = hf * BLK + (2 * g + c) * P
                            for k in range(4):
                                last = pe.matmul(bank[:, c * SEQ:(c + 1) * SEQ], w[:, k, col:col + P],
                                                 yaT[:, k, :], start=(k == 0), stop=(k == 3))
                        last.then_inc(d_full, 1)
                pe.wait_ge(d_full, l * ND + D_FILLS.index(("br", 0, 1, 1)) + 1)
                pe.sem_inc(w_used, 1)
                pe.wait_ge(xl_done, (l + 1) * 4 * NT)
                for hf in range(2):
                    for c in range(QUARTERS):
                        n = QUARTERS * (N_IN + hf) + c
                        _, hi, lo = granule(n)
                        if c % 2 == 0:
                            bank = d_start("br", 1, hf, c // 2)
                        pe.wait_ge(lo_done, l * N_GRAN + n + 1)
                        o = bank[:, (c % 2) * SEQ:(c % 2 + 1) * SEQ]
                        for k in range(KD):
                            last = split_product(o, (hi[:, k, :], lo[:, k, :]), (xh[:, k, :], xl[:, k, :]),
                                                 k == 0, k == KD - 1)
                        last.then_inc(d_full if c % 2 else g_used, 1)
                d_ready("br", 1, 1, 1)
                for t in range(NT):
                    for hf in range(2):
                        bank = d_start("mix", hf, t)
                        pe.wait_ge(wo_in[hf], 16 * l + 16)
                        for k in range(KD):
                            last = pe.matmul(bank, mergedT[:, k, t * P:(t + 1) * P], wo[hf][:, k, :],
                                             start=(k == 0), stop=(k == KD - 1))
                        last.then_inc(d_full, 1)
                def x1_transposes(t):
                    pe.wait_ge(ln1_done, l * NT + t + 1)
                    for g in range(2):
                        bank = a_start("x1T", t, g)
                        transposes([xs[:, t, (4 * g + c) * P:(4 * g + c + 1) * P] for c in range(4)],
                                   bank).then_inc(a_full, 1)
                    a_ready("x1T", t, 1)

                nq, ns = 2 + len(QUERY_STEPS), len(QUERY_STEPS)
                x1_transposes(0)
                keys = keys_sb[:, :].rearrange("p (q d) -> p q d", q=2)
                pe.wait_ge(keys_in, 16 * l + 16)
                for q in range(2):
                    pe.wait_ge(q_used, l * nq + q + 1)
                    pe.transpose(banks[:, q, 0:NKEY], keys[:, q, :], ident).then_inc(q_full, 1)

                def queries(n):
                    hp, chunks = QUERY_STEPS[n]
                    tok = slice(chunks[0] * P, (chunks[-1] + 1) * P)
                    w = unit_in("query", hp // 4)
                    pe.wait_ge(q_used, l * nq + 2 + n + 1)
                    for k in range(KD):
                        last = pe.matmul(banks[:, n % 2, tok], w[:, k, (hp % 4) * P:(hp % 4 + 1) * P],
                                         xT[:, k, tok], start=(k == 0), stop=(k == KD - 1))
                    last.then_inc(q_full, 1)
                    if hp % 4 == 3 and chunks[-1] == NT - 1:
                        pe.wait_ge(q_full, l * nq + 2 + n + 1)
                        pe.sem_inc(w_used, 1)

                def head_scores(n):
                    hp, chunks = QUERY_STEPS[n]
                    pe.wait_ge(q_used, l * nq + 2 + n + 3)
                    pe.wait_ge(s_used, l * (ns + 2) + n + 1)
                    for c in chunks:
                        last = pe.matmul(banks[:, 2 + n % 2, c * NKEY:(c + 1) * NKEY],
                                         qT_ring[:, n % 2, c * P:(c + 1) * P], key_T[:, hp % 2, :],
                                         start=True, stop=True)
                    last.then_inc(s_full, 1)

                for n, (hp, chunks) in enumerate(QUERY_STEPS):
                    if n == 4:
                        x1_transposes(1)
                    queries(n)
                    if n == 1:
                        d_ready("mix", 1, 1)
                    if n >= 1:
                        head_scores(n - 1)
                head_scores(ns - 1)

                for c in range(NT):
                    pe.wait_ge(acc_free, l * NT + c + 1)
                    for hf in range(2):
                        pe.matmul(acc[:, hf, :], alpha_i, xs[:, c, hf * BLK:(hf + 1) * BLK], start=True, stop=False)

                    def sum_head(i, closes=False):
                        for j in range(NSEL):
                            pe.wait_ge(diag_done, i * NSEL + j + 2)
                            pe.wait_ge(v_in[j % U_RING], i * (16 * NSEL // U_RING) + 16 * (j // U_RING + 1))
                            for hf in range(2):
                                last = pe.matmul(acc[:, hf, :], diags[:, j % DIAGS, :],
                                                 v_rows[:, j % U_RING, hf * BLK:(hf + 1) * BLK],
                                                 start=False, stop=closes and j == NSEL - 1)
                            last.then_inc(v_used, 1)

                    with pe.Fori(c * PH, (c + 1) * PH - 1) as h:
                        sum_head(l * HEADS + h)
                    sum_head(l * HEADS + (c + 1) * PH - 1, closes=True)

        @block.scalar
        def _(act):
            act.sem_inc(a_used, 4)
            act.sem_inc(q_used, 2)
            act.sem_inc(s_used, 2)
            act.sem_inc(fexp_done, 1)
            act.sem_inc(diag_done, 1)
            act.wait_ge(const_in, 32)
            act.wait_ge(w_in_sem[0], 16)
            act.dma_start(const_sb[:, P:], consts[:, P:]).then_inc(tables_in, 16)
            with act.Fori(0, DEPTH) as l:
                def a_wait(*name):
                    act.wait_ge(a_full, l * NA + A_FILLS.index(name) + 1)
                    return a_bank(*name)

                def copy(dst, src, sem_):
                    act.activation(dst, src, ACT.Copy).then_inc(sem_, 1)

                def four(bank):
                    return bank.rearrange("p (c s) -> p c s", c=4)

                def norm_parameters(*prms):
                    for n, prm in enumerate(prms):
                        act.dma_start(lnp[:, n, :], prm[l].partition_broadcast(P)).then_inc(lnp_in, 16)

                def hi_parts(first, end):
                    for n in range(first, end):
                        w, hi, _ = granule(n)
                        k = SPLIT[n // QUARTERS]
                        if n % QUARTERS == 0:
                            act.wait_ge(w_in_sem[k % W_RING], l * W_TURN + 16 * (k // W_RING + 1))
                        if n >= G_RING:
                            end_sem, count = granule_end(n - G_RING)
                            done, per_layer = {"d": (d_full, ND), "a": (a_full, NA), "g": (g_used, N_G_USED)}[end_sem]
                            act.wait_ge(done, l * per_layer + count)
                        act.activation(hi, w, ACT.Copy).then_inc(hi_done, 1)

                hi_parts(0, 1)
                act.wait_ge(ln2_done, l * NT + 1)
                norm_parameters(ln1_g, ln1_b)
                def split_transposed(name, whole):
                    for t in range(NT):
                        for g in range(2):
                            at = (slice(None), slice(4 * g, 4 * g + 4), slice(t * P, (t + 1) * P))
                            bank = four(a_wait(name, t, g))
                            act.activation(xh[at], bank, ACT.Copy)
                            copy(whole[at], bank, a_used)

                split_transposed("xT", xT)
                hi_parts(1, 15)
                for t in range(NT):
                    copy(va[:, t, :], a_wait("v_a", t), a_used)
                for dst, name in ((qaT, "qaT"), (kaT, "kaT")):
                    for t in range(NT):
                        copy(dst[:, :, t * P:(t + 1) * P], four(a_wait(name, t)), a_used)
                hi_parts(15, 19)
                for t, p in ((0, p0), (1, p1)):
                    act.wait_ge(max_ready, l * NT + t + 1)
                    for h in range(MH):
                        if h % 3 == 2:
                            n = 19 + 2 * t + h // 3
                            hi_parts(n, n + 1)
                        act.activation(p[:, h, :], p[:, h, :], ACT.Exp, bias=negmax[:, t * MH + h:t * MH + h + 1],
                                       accum_out=rsum[:, t * MH + h:t * MH + h + 1]).then_inc(exp_ready, 1)
                for hf in range(2):
                    hi_parts(23 + 4 * hf, 27 + 4 * hf)
                    for t in range(NT):
                        copy(vr[:, t, hf * BLK:(hf + 1) * BLK], a_wait(f"v_r{hf}", t), a_used)
                for dst, name in ((qrT, "qrT"), (krT, "krT")):
                    for t in range(NT):
                        copy(dst[:, :, t * P:(t + 1) * P], four(a_wait(name, t)), a_used)
                for g in range(2):
                    copy(pT0[:, 4 * g:4 * g + 4, 0:P], four(a_wait("pT0", g)), a_used)
                for g in range(4):
                    bank = four(a_wait("pT1", g))
                    act.activation(pT0[:, 2 * g:2 * g + 2, P:SEQ], bank[:, 0::2, :], ACT.Copy)
                    copy(pT1[:, 2 * g:2 * g + 2, :], bank[:, 1::2, :], a_used)
                for hf in range(2):
                    hi_parts(31 + 4 * hf, 35 + 4 * hf)
                    for t in range(NT):
                        act.wait_ge(d_full, l * ND + D_FILLS.index((f"g_r{hf}", t)) + 1)
                        act.activation(gr[:, t, hf * BLK:(hf + 1) * BLK], d_bank(f"g_r{hf}", t), ACT.Tanh,
                                       scale=0.5).then_inc(th_ready, 1)
                for t in range(NT):
                    for g in range(2):
                        copy(yaT[:, 2 * g:2 * g + 2, t * P:(t + 1) * P],
                             four(a_wait("yaT", t, g))[:, 0:2, :], a_used)
                for b in range(4):
                    for g in range(2):
                        n = QUARTERS * (FIRST_GATE + b) + 2 * g + G_RING
                        hi_parts(n, min(n + 2, QUARTERS * N_IN))
                        bank = a_wait("gate", b, g)
                        act.activation(gT[:, 4 * b + 2 * g:4 * b + 2 * g + 2, :],
                                       bank.rearrange("p (c s) -> p c s", c=2), ACT.Tanh,
                                       scale=0.5).then_inc(a_used, 1)
                def transposed(name, dst, t):
                    for g in range(2):
                        copy(dst[:, 4 * g:4 * g + 4, t * P:(t + 1) * P], four(a_wait(name, t, g)), a_used)

                split_transposed("yrT", yrT)
                hi_parts(QUARTERS * N_IN, N_GRAN)

                nq, ns = 2 + len(QUERY_STEPS), len(QUERY_STEPS)
                transposed("x1T", xT, 0)
                for q in range(2):
                    act.wait_ge(q_full, l * nq + q + 1)
                    copy(key_T[:, q, :], banks[:, q, 0:NKEY], q_used)
                by_head = scores.rearrange("p (c h k) -> p c h k", c=NT, k=NKEY)

                def query_out(n):
                    chunks = QUERY_STEPS[n][1]
                    tok = slice(chunks[0] * P, (chunks[-1] + 1) * P)
                    act.wait_ge(q_full, l * nq + 2 + n + 1)
                    if n >= 2:
                        act.wait_ge(s_full, l * ns + n - 1)
                    copy(qT_ring[:, n % 2, tok], banks[:, n % 2, tok], q_used)

                def scores_out(n):
                    hp, chunks = QUERY_STEPS[n]
                    cs = slice(chunks[0], chunks[-1] + 1)
                    act.wait_ge(s_full, l * ns + n + 1)
                    copy(by_head[:, cs, hp, :],
                         banks[:, 2 + n % 2, 0:NT * NKEY].rearrange("p (c k) -> p c k", c=NT)[:, cs, :], s_used)

                def final_exp(i):
                    act.wait_ge(sel_done, i + 1)
                    act.activation(gexp, fs, ACT.Exp, bias=negmax[:, 0:1], accum_out=gsum).then_inc(fexp_done, 1)

                def tanh_of(i):
                    act.wait_ge(pre_done, i + 1)
                    act.activation(hth, hx, ACT.Tanh, scale=GELU_C).then_inc(tanh_done, 1)

                def diagonals(i):
                    for j in range(NSEL):
                        act.wait_ge(v_used, i * NSEL + j + 1 + U_RING - DIAGS)
                        act.activation(diags[:, j % DIAGS, :], ident, ACT.Copy,
                                       scale=wts[:, j:j + 1]).then_inc(diag_done, 1)

                for n in range(ns):
                    if n == 4:
                        transposed("x1T", xT, 1)
                        norm_parameters(ln2_g, ln2_b)
                    query_out(n)
                    if n >= 1:
                        scores_out(n - 1)
                    if n == FIRST_EXP:
                        final_exp(l * HEADS)
                scores_out(ns - 1)
                act.drain().then_inc(s_used, 2)
                with act.Fori(0, HEADS - 1) as h:
                    i = l * HEADS + h
                    tanh_of(i)
                    act.wait_ge(wts_done, i + 1)
                    final_exp(i + 1)
                    diagonals(i)
                last = l * HEADS + HEADS - 1
                tanh_of(last)
                act.wait_ge(wts_done, last + 1)
                diagonals(last)

        @block.vector
        def _(dve):
            def settle():
                dve.drain()

            def rsqrt(n, eps, gain):
                v, y, t = nv[:, 0:n], ny[:, 0:n], nt[:, 0:n]
                settle()
                dve.tensor_scalar(v, mv[:, 0:n, 1], eps, None, ALU.add)
                settle()
                dve.tensor_scalar(t.bitcast(I32), v.bitcast(I32), 1, None, ALU.logical_shift_right)
                settle()
                dve.tensor_scalar(y.bitcast(I32), t.bitcast(I32), -1.0, float(0x5F3759DF), ALU.mult, ALU.add)
                dve.tensor_scalar(v, v, -0.5, None, ALU.mult)
                settle()
                for step in range(3):
                    if n == 1:
                        dve.tensor_scalar(t, y, y, v, ALU.mult, ALU.mult)
                    else:
                        dve.tensor_tensor(t, y, y, ALU.mult)
                        settle()
                        dve.tensor_tensor(t, t, v, ALU.mult)
                    settle()
                    dve.scalar_tensor_tensor(y, t, 1.5, y, ALU.add, ALU.mult)
                    settle()
                if gain != 1.0:
                    dve.tensor_scalar(y, y, gain, None, ALU.mult)
                    settle()

            dve.memset(lbase, 0.0)
            dve.sem_inc(d_used, 4)
            dve.sem_inc(ln2_done, 1)
            dve.sem_inc(u_used, U_RING)
            dve.sem_inc(acc_free, 1)
            dve.sem_inc(idx_taken, 1)
            dve.wait_ge(const_in, 32)
            with dve.Fori(0, DEPTH) as l:
                def d_wait(*name):
                    dve.wait_ge(d_full, l * ND + D_FILLS.index(name) + 1)
                    return d_bank(*name)

                def rope(src, t, heads, view, cos, sin):
                    bank = d_wait(src, t)
                    o = rot[:, rot_slot(src, t), :]
                    n = BLK // heads
                    cosb = cos[:, t, :].unsqueeze(1).to_broadcast([P, heads, n])
                    dve.tensor_tensor(o.rearrange("p (h c) -> p h c", h=heads),
                                      bank.rearrange("p (h c) -> p h c", h=heads), cosb, ALU.mult)
                    s = sin[:, t, :].unsqueeze(1).to_broadcast([P, heads, n])
                    for half in range(2):
                        dve.tensor_tensor(view(t512[:, :].rearrange("p (h c) -> p h c", h=heads), half),
                                          view(bank.rearrange("p (h c) -> p h c", h=heads), 1 - half),
                                          view(s, half), ALU.mult)
                    settle()
                    dve.tensor_tensor(o, o, t512[:, :], ALU.add).then_inc(d_used, 1)
                    settle()

                def halves(a, half):
                    n = a.shape[-1] // 2
                    return a[:, :, half * n:(half + 1) * n]

                def pairs(a, half):
                    return a[:, :, half::2]

                def lo_parts(name, whole):
                    for t in range(NT):
                        for g in range(2):
                            at = (slice(None), slice(4 * g, 4 * g + 4), slice(t * P, (t + 1) * P))
                            dve.wait_ge(a_used, l * NA + A_FILLS.index((name, t, g)) + 5)
                            dve.tensor_tensor(xl[at], whole[at], xh[at].bitcast(F32),
                                              ALU.subtract).then_inc(xl_done, 1)

                lo_parts("xT", xT)
                dve.wait_ge(tables_in, 16)
                for t in range(NT):
                    rope("q_a", t, MH, halves, cos_a, sin_a)
                for t in range(NT):
                    rope("k_a", t, MH, halves, cos_a, sin_a)
                dve.wait_ge(a_full, l * NA + A_FILLS.index(("qaT", 1)) + 1)
                for t in range(NT):
                    rope("q_r", t, RH, pairs, cos_r, sin_r)
                for t, p, per in ((0, p0, 4), (1, p1, 2)):
                    keys = (t + 1) * P
                    m = mask[:, (1 - t) * P:2 * P].unsqueeze(1).to_broadcast([P, per, keys])
                    for g in range(MH // per):
                        bank = d_wait(f"s{t}", g)
                        first = head_of(t, g, 0)
                        dve.scalar_tensor_tensor(p[:, first:first + 2 * per - 1:2, :],
                                                 bank.rearrange("p (h k) -> p h k", h=per), SCALE, m,
                                                 ALU.mult, ALU.add).then_inc(d_used, 1)
                    settle()
                    dve.tensor_reduce(negmax[:, t * MH:(t + 1) * MH], p, AX_X, ALU.max,
                                      negate=True).then_inc(max_ready, 1)
                dve.wait_ge(a_full, l * NA + A_FILLS.index(("kaT", 1)) + 1)
                for t in range(NT):
                    rope("k_r", t, RH, pairs, cos_r, sin_r)
                for g in range(2):
                    bank = d_wait("sc0", g)
                    dve.tensor_tensor(sc0[:, 2 * g:2 * g + 2, :], bank.rearrange("p (h n) -> p h n", h=2),
                                      decay[:, 2 * g:2 * g + 2, :], ALU.mult).then_inc(d_used, 1)
                for g in range(2):
                    bank = d_wait("sc1", g)
                    dve.tensor_tensor(sc1[:, 2 * g:2 * g + 2, :],
                                      bank[:, 0:2 * P].rearrange("p (h n) -> p h n", h=2),
                                      decay[:, 2 * g:2 * g + 2, 0:P], ALU.mult).then_inc(d_used, 1)
                for hf in range(2):
                    for t in range(NT):
                        o = gr[:, t, hf * BLK:(hf + 1) * BLK]
                        dve.wait_ge(th_ready, l * 2 * NT + hf * NT + t + 1)
                        dve.scalar_tensor_tensor(o, o, 1.0, d_wait(f"g_r{hf}", t), ALU.add,
                                                 ALU.mult).then_inc(d_used, 1)
                dve.reciprocal(rinv, rsum)
                settle()
                for t in range(NT):
                    bank = d_wait("ya", t)
                    r = rinv[:, t * MH:(t + 1) * MH].unsqueeze(2).to_broadcast([P, MH, MD])
                    dve.tensor_tensor(ya[:, t, :].rearrange("p (h c) -> p h c", h=MH),
                                      bank.rearrange("p (h c) -> p h c", h=MH), r, ALU.mult).then_inc(d_used, 1)
                for t in range(NT):
                    for h in range(RH):
                        bank = d_wait("yr", t, h // 2)
                        dve.bn_stats(stats[:, t * RH + h, :], bank[:, (h % 2) * RV:(h % 2 + 1) * RV])
                settle()
                for n in range(NT * RH):
                    dve.bn_aggr(mv[:, n, :], stats[:, n, :])
                rsqrt(NT * RH, EPS, 0.5)
                for t in range(NT):
                    for h in range(RH):
                        n = t * RH + h
                        bank = d_bank("yr", t, h // 2)
                        o = gr[:, t, h * RV:(h + 1) * RV]
                        tmp = t512[:, (h % 2) * RV:(h % 2 + 1) * RV]
                        read = dve.tensor_scalar(tmp, bank[:, (h % 2) * RV:(h % 2 + 1) * RV], mv[:, n, 0:1],
                                                 ny[:, n:n + 1], ALU.subtract, ALU.mult)
                        settle()
                        done = dve.tensor_tensor(o, o, tmp, ALU.mult)
                        if h % 2:
                            done.then_inc(d_used, 1)
                            settle()
                lo_parts("yrT", yrT)
                dve.wait_ge(a_used, l * NA + A_FILLS.index(("gate", 3, 1)) + 5)
                dve.wait_ge(a_full, l * NA + A_FILLS.index(("krT", 1)) + 1)
                for which in range(2):
                    for hf in range(2):
                        for g in range(2):
                            c = 4 * hf + 2 * g
                            o = mergedT[:, c:c + 2, :]
                            b = d_wait("br", which, hf, g).rearrange("p (c s) -> p c s", c=2)
                            gate = gT[:, KD * which + c:KD * which + c + 2, :]
                            if which == 0:
                                dve.scalar_tensor_tensor(o, gate, 1.0, b, ALU.add, ALU.mult).then_inc(d_used, 1)
                            else:
                                o2 = t512[:, :].rearrange("p (c s) -> p c s", c=2)
                                dve.scalar_tensor_tensor(o2, gate, 1.0, b, ALU.add, ALU.mult)
                                settle()
                                dve.tensor_tensor(o, o, o2, ALU.add).then_inc(d_used, 1)
                                settle()
                dve.wait_ge(lnp_in, 64 * l + 32)
                for t in range(NT):
                    for hf in range(2):
                        o = xs[:, t, hf * BLK:(hf + 1) * BLK]
                        dve.scalar_tensor_tensor(o, o, 2.0 * ALPHA, d_wait("mix", hf, t), ALU.mult,
                                                 ALU.add).then_inc(d_used, 1)
                        settle()
                        dve.bn_stats(stats[:, hf, :], o)
                    settle()
                    dve.bn_aggr(mv[:, 0, :], stats[:, 0:2, :])
                    rsqrt(1, 4.0 * EPS, 1.0)
                    o = xs[:, t, :]
                    dve.scalar_tensor_tensor(o, o, mv[:, 0, 0:1], lnp[:, 0, :], ALU.subtract, ALU.mult)
                    settle()
                    dve.scalar_tensor_tensor(o, o, ny[:, 0:1], lnp[:, 1, :], ALU.mult, ALU.add).then_inc(ln1_done, 1)
                settle()

                def select(i, h, fresh=None):
                    if fresh is not None:
                        dve.wait_ge(s_used, l * (len(QUERY_STEPS) + 2) + fresh)
                    dve.tensor_copy(cur.rearrange("p q k -> p (q k)"), scores[:, bass.ds(h * 2 * NKEY, 2 * NKEY)])
                    settle()
                    for q in range(2):
                        dve.max(top[:, q, 0:8], cur[:, q, :])
                    settle()
                    for q in range(2):
                        dve.max_index(tidx[:, q, 0:8], top[:, q, 0:8], cur[:, q, :])
                        dve.match_replace(cur2[:, q, :], top[:, q, 0:8], cur[:, q, :], LOWEST)
                    settle()
                    for q in range(2):
                        dve.max(top[:, q, 8:16], cur2[:, q, :])
                    settle()
                    for q in range(2):
                        dve.max_index(tidx[:, q, 8:16], top[:, q, 8:16], cur2[:, q, :])
                    pair = [P, NSEL, NSEL]
                    dve.tensor_tensor(cand.rearrange("p (a b) -> p a b", a=NSEL),
                                      top[:, 0, :].unsqueeze(2).to_broadcast(pair),
                                      top[:, 1, :].unsqueeze(1).to_broadcast(pair), ALU.add)
                    settle()
                    dve.wait_ge(fexp_done, i + 1)
                    dve.tensor_copy(tidxf, tidx)
                    dve.max(fs[:, 0:8], cand)
                    settle()
                    dve.max_index(pos[:, 0:8], fs[:, 0:8], cand)
                    dve.match_replace(cand2, fs[:, 0:8], cand, LOWEST)
                    settle()
                    dve.max(fs[:, 8:16], cand2)
                    dve.tensor_scalar(negmax[:, 0:1], fs[:, 0:1], -1.0, None, ALU.mult)
                    settle()
                    dve.max_index(pos[:, 8:16], fs[:, 8:16], cand2)
                    settle()
                    dve.tensor_scalar(pos2[:, 0, :], pos, 4, None, ALU.logical_shift_right)
                    dve.tensor_scalar(pos2[:, 1, :], pos, NSEL - 1, None, ALU.bitwise_and)
                    settle()
                    dve.tensor_copy(posf, pos2)
                    settle()
                    for q in range(2):
                        dve.tensor_tensor(onehot4[:, q, :, :], posf[:, q, :].unsqueeze(2).to_broadcast(pair),
                                          iota.unsqueeze(1).to_broadcast(pair), ALU.is_equal)
                    settle()
                    for q in range(2):
                        dve.tensor_tensor(onehot4[:, q, :, :], onehot4[:, q, :, :],
                                          tidxf[:, q, :].unsqueeze(1).to_broadcast(pair), ALU.mult)
                    settle()
                    dve.tensor_reduce(picked, onehot4, AX_X, ALU.add)
                    settle()
                    dve.tensor_scalar(picked[:, 0, :], picked[:, 0, :], float(NKEY), lbase, ALU.mult, ALU.add)
                    settle()
                    dve.wait_ge(idx_taken, i + 1)
                    dve.tensor_tensor(idx_next, picked[:, 0, :], picked[:, 1, :], ALU.add).then_inc(sel_done, 1)

                def dots(i):
                    for j in range(NSEL):
                        dve.wait_ge(u_in[j % U_RING], i * (16 * NSEL // U_RING) + 16 * (j // U_RING + 1))
                        row = u_rows[:, j % U_RING, :]
                        dve.tensor_tensor_reduce(out=row, in0=row, in1=x_ps, scale=1.0, scalar=0.0, op0=ALU.mult,
                                                 op1=ALU.add, accum_out=hd[:, j:j + 1]).then_inc(u_used, 1)
                    settle()

                def weights(i):
                    dve.tensor_tensor(hx, hd, hd, ALU.mult)
                    dve.wait_ge(fexp_done, i + 2)
                    dve.reciprocal(ginv, gsum)
                    settle()
                    dve.tensor_scalar(hx, hx, GELU_A, 1.0, ALU.mult, ALU.add)
                    dve.tensor_scalar(gh, gexp, ginv, 0.5, ALU.mult, ALU.mult)
                    settle()
                    dve.tensor_tensor(hx, hx, hd, ALU.mult).then_inc(pre_done, 1)
                    dve.tensor_tensor(gh, gh, hd, ALU.mult)
                    settle()
                    dve.wait_ge(tanh_done, i + 1)
                    dve.wait_ge(diag_done, i * NSEL + 1)
                    dve.scalar_tensor_tensor(wts, hth, 1.0, gh, ALU.add, ALU.mult).then_inc(wts_done, 1)

                def dot_operand(c):
                    dve.tensor_copy(x_ps, xs[:, c, :])
                    settle()

                def second_norm(c):
                    dve.wait_ge(lnp_in, 64 * l + 64)
                    dve.wait_ge(v_used, (l * HEADS + (c + 1) * PH) * NSEL + U_RING)
                    for hf in range(2):
                        dve.bn_stats(stats[:, hf, :], acc[:, hf, :])
                    settle()
                    dve.bn_aggr(mv[:, 0, :], stats[:, 0:2, :])
                    rsqrt(1, EPS, 1.0)
                    o = xs[:, c, :]
                    dve.scalar_tensor_tensor(o, acc.rearrange("p a n -> p (a n)"), mv[:, 0, 0:1], lnp[:, 0, :],
                                             ALU.subtract, ALU.mult).then_inc(acc_free, 1)
                    settle()
                    dve.scalar_tensor_tensor(o, o, ny[:, 0:1], lnp[:, 1, :], ALU.mult, ALU.add).then_inc(ln2_done, 1)

                base = l * HEADS
                select(base, 0, fresh=4)
                dve.wait_ge(a_used, l * NA + NA + 4)
                dot_operand(0)
                select(base + 1, 1, fresh=6)
                dots(base)
                weights(base)
                with dve.Fori(1, PH) as h:
                    select(base + h + 1, h + 1, fresh=2 * h + 10)
                    dots(base + h)
                    weights(base + h)
                dot_operand(1)
                select(base + PH + 1, PH + 1)
                dots(base + PH)
                weights(base + PH)
                second_norm(0)
                with dve.Fori(PH + 1, HEADS - 1) as h:
                    select(base + h + 1, h + 1)
                    dots(base + h)
                    weights(base + h)
                dots(base + HEADS - 1)
                weights(base + HEADS - 1)
                second_norm(1)
                dve.tensor_scalar(lbase, lbase, float(NEXP), None, ALU.add)
                settle()


def shape_constants():
    import numpy as np
    f = np.float32
    c = np.zeros((P, N_CONST), f)

    def put(name, a):
        o, w = CONSTS[name]
        c[:, o:o + w] = np.asarray(a).reshape(P, w)

    put("ident", np.eye(P))
    put("alpha_i", ALPHA * np.eye(P))
    q, k = np.arange(P)[:, None], np.arange(P)[None, :]
    put("mask", np.concatenate([np.zeros((P, P)), np.where(k <= q, 0.0, -1e30)], 1))
    log_g = np.log(1.0 - 2.0 ** (-5.0 - np.arange(RH)))
    diff = np.arange(SEQ)[None, None, :] - np.arange(P)[:, None, None]
    put("decay", np.where(diff >= 0, np.exp(log_g[None, :, None] * np.maximum(diff, 0)), 0.0) * RK ** -0.5)
    pos = (np.arange(NT)[None, :, None] * P + np.arange(P)[:, None, None]).astype(f)
    ang = pos * (f(10000.0) ** (-np.arange(0, MD, 2, dtype=f) / f(MD)))
    put("cos_a", np.concatenate([np.cos(ang), np.cos(ang)], -1))
    put("sin_a", np.concatenate([-np.sin(ang), np.sin(ang)], -1))
    ang = pos * (f(1.0) / f(10000.0) ** np.linspace(0.0, 1.0, RK // 2, dtype=f))
    put("cos_r", np.repeat(np.cos(ang), 2, -1))
    put("sin_r", np.stack([-np.sin(ang), np.sin(ang)], -1))
    put("iota", np.broadcast_to(np.arange(NSEL), (P, NSEL)))
    return c


def kernel(**inputs):
    import numpy as np
    import concourse.bacc as bacc
    from concourse.bass_utils import run_bass_kernel_spmd as run

    names = ["x", "w_in", "w_moba_out", "w_ret_out", "w_out", "ln1_g", "ln1_b", "peer_w_query", "peer_sub_keys",
             "peer_u", "peer_v", "ln2_g", "ln2_b"]
    nc = bacc.Bacc("TRN2", target_bir_lowering=False, num_devices=1)
    arrays = {f"in_{n}": np.ascontiguousarray(inputs[n]) for n in names}
    arrays["in_consts"] = shape_constants()
    args = [nc.dram_tensor(n, a.shape, mybir.dt.from_np(a.dtype), kind="ExternalInput").ap()
            for n, a in arrays.items()]
    out = nc.dram_tensor("out", (1, SEQ, D), F32, kind="ExternalOutput").ap()
    build(nc, *args, out)
    return run(nc, [arrays], core_ids=[0]).results[0]["out"]
```
